# Optimizing a Trainium2 kernel written in Bass

```python
import jax, jax.numpy as jnp
from jax import lax
import numpy as np

D_MODEL = 1024
BATCH = 1
SEQ = 1024
DEPTH = 1
DEC_BATCH = 8
DEC_SEQ = 8
PAST_LEN = 1024
PAGE_SIZE = 128

D_CONV = D_MODEL // 2
CONV_WIDTH = 3
N_HEADS = 8
HEAD_DIM = 64
D_ATT = N_HEADS * HEAD_DIM
D_FF = 4 * D_MODEL
Q_BLOCK = 128
RMS_EPS = 1e-6
SB_BIAS_INIT = -8.0
SPLIT_POINTS = (D_CONV, 2 * D_CONV, 3 * D_CONV,
                3 * D_CONV + D_ATT, 3 * D_CONV + 2 * D_ATT, 3 * D_CONV + 3 * D_ATT,
                3 * D_CONV + 3 * D_ATT + D_MODEL)
D_IN = 3 * D_CONV + 3 * D_ATT + 2 * D_MODEL

kernel_name = "hybrid_shortconv_stickbreaking_step"

def rmsnorm(x, w):
    xf = x.astype(jnp.float32)
    y = xf * lax.rsqrt(jnp.mean(xf * xf, axis=-1, keepdims=True) + RMS_EPS)
    return (y * w.astype(jnp.float32)).astype(x.dtype)

def stick_breaking_block(q, k, v, bias, q_pos, k_pos):
    z = (jnp.einsum('bhqd,bhkd->bhqk', q, k).astype(jnp.float32) * (HEAD_DIM ** -0.5)
         + bias.astype(jnp.float32)[None, :, None, None])
    causal = k_pos[None, :] < q_pos[:, None]
    log_beta = jax.nn.log_sigmoid(z)
    log_stay = jnp.where(causal, log_beta - z, 0.0)
    log_after = lax.cumsum(log_stay, axis=3, reverse=True) - log_stay
    w = jnp.where(causal, jnp.exp(log_beta + log_after), 0.0)
    return jnp.einsum('bhqk,bhkd->bhqd', w.astype(v.dtype), v)

def sb_prompt(q, k, v, bias):
    B, S = q.shape[0], q.shape[1]
    nb = S // Q_BLOCK
    qb = q.reshape(B, nb, Q_BLOCK, N_HEADS, HEAD_DIM).transpose(1, 0, 3, 2, 4)
    kt = k.transpose(0, 2, 1, 3)
    vt = v.transpose(0, 2, 1, 3)
    k_pos = jnp.arange(S)

    def one_block(args):
        q_blk, i = args
        q_pos = i * Q_BLOCK + jnp.arange(Q_BLOCK)
        return stick_breaking_block(q_blk, kt, vt, bias, q_pos, k_pos)

    o = lax.map(one_block, (qb, jnp.arange(nb)))
    return o.transpose(1, 0, 3, 2, 4).reshape(B, S, D_ATT)

def sb_sample(q, k_new, v_new, k_past, v_past, bias):
    B, L = q.shape[0], q.shape[1]
    P = k_past.shape[1]
    kt = jnp.concatenate([k_past, k_new], axis=1).transpose(0, 2, 1, 3)
    vt = jnp.concatenate([v_past, v_new], axis=1).transpose(0, 2, 1, 3)
    q_pos = P + jnp.arange(L)
    k_pos = jnp.arange(P + L)
    o = stick_breaking_block(q.transpose(0, 2, 1, 3), kt, vt, bias, q_pos, k_pos)
    return o.transpose(0, 2, 1, 3).reshape(B, L, D_ATT)

def hybrid_layer(x, conv_prev, k_past, v_past, norm1_w, w_in, conv_w, w_proj_conv,
                 w_proj_attn, att_bias, w_out, norm2_w, w_up, w_down):
    B, L = x.shape[0], x.shape[1]
    h = rmsnorm(x, norm1_w)
    proj = h @ w_in
    b_g, c_g, u, q, k, v, gate_conv, gate_att = jnp.split(proj, SPLIT_POINTS, axis=-1)
    cu = c_g * u
    cu_full = jnp.concatenate([conv_prev, cu], axis=1)
    conv = sum(conv_w[j] * cu_full[:, j:j + L] for j in range(CONV_WIDTH))
    y_conv = (b_g * conv) @ w_proj_conv
    new_conv = cu_full[:, L:]
    q = q.reshape(B, L, N_HEADS, HEAD_DIM)
    k = k.reshape(B, L, N_HEADS, HEAD_DIM)
    v = v.reshape(B, L, N_HEADS, HEAD_DIM)
    if k_past is None:
        o = sb_prompt(q, k, v, att_bias)
    else:
        o = sb_sample(q, k, v, k_past, v_past, att_bias)
    y_att = o @ w_proj_attn
    merged = jax.nn.sigmoid(gate_conv) * y_conv + jax.nn.sigmoid(gate_att) * y_att
    x = x + merged @ w_out
    f = rmsnorm(x, norm2_w) @ w_up
    x = x + jnp.square(jax.nn.relu(f)) @ w_down
    return x, new_conv, k, v

def setup_inputs(seed: int = 0) -> dict:
    key = jax.random.key(seed)
    ks = jax.random.split(key, 20)
    n_pages = PAST_LEN // PAGE_SIZE
    n_used = DEC_BATCH * n_pages
    n_pool = n_used + n_used // 4
    f32 = jnp.float32
    x_prompt = jax.random.normal(ks[0], (BATCH, SEQ, D_MODEL), f32)
    x_sample = jax.random.normal(ks[1], (DEC_BATCH, DEC_SEQ, D_MODEL), f32)
    cache_k = jax.random.normal(ks[2], (DEPTH, n_pool, PAGE_SIZE, N_HEADS, HEAD_DIM), f32)
    cache_v = jax.random.normal(ks[3], (DEPTH, n_pool, PAGE_SIZE, N_HEADS, HEAD_DIM), f32)
    state_conv = jax.random.normal(ks[4], (DEPTH, DEC_BATCH, CONV_WIDTH - 1, D_CONV), f32)
    page_table = jax.random.permutation(ks[5], n_pool)[:n_used].astype(jnp.int32).reshape(DEC_BATCH, n_pages)
    norm1_w = 1.0 + 0.02 * jax.random.normal(ks[6], (DEPTH, D_MODEL), f32)
    w_in = jax.random.normal(ks[7], (DEPTH, D_MODEL, D_IN), f32) * D_MODEL ** -0.5
    conv_w = jax.random.normal(ks[8], (DEPTH, CONV_WIDTH, D_CONV), f32) * CONV_WIDTH ** -0.5
    w_proj_conv = jax.random.normal(ks[9], (DEPTH, D_CONV, D_MODEL), f32) * D_CONV ** -0.5
    w_proj_attn = jax.random.normal(ks[10], (DEPTH, D_ATT, D_MODEL), f32) * D_ATT ** -0.5
    att_bias = SB_BIAS_INIT + 0.1 * jax.random.normal(ks[16], (DEPTH, N_HEADS), f32)
    w_out = jax.random.normal(ks[11], (DEPTH, D_MODEL, D_MODEL), f32) * D_MODEL ** -0.5
    norm2_w = 1.0 + 0.02 * jax.random.normal(ks[12], (DEPTH, D_MODEL), f32)
    w_up = jax.random.normal(ks[13], (DEPTH, D_MODEL, D_FF), f32) * D_MODEL ** -0.5
    w_down = jax.random.normal(ks[14], (DEPTH, D_FF, D_MODEL), f32) * D_FF ** -0.5
    norm_f_w = 1.0 + 0.02 * jax.random.normal(ks[15], (D_MODEL,), f32)
    return {"x_prompt": x_prompt, "x_sample": x_sample, "cache_k": cache_k, "cache_v": cache_v,
            "state_conv": state_conv, "page_table": page_table, "norm1_w": norm1_w, "w_in": w_in,
            "conv_w": conv_w, "w_proj_conv": w_proj_conv, "w_proj_attn": w_proj_attn,
            "att_bias": att_bias, "w_out": w_out,
            "norm2_w": norm2_w, "w_up": w_up, "w_down": w_down, "norm_f_w": norm_f_w}

def reference(x_prompt, x_sample, cache_k, cache_v, state_conv, page_table, norm1_w, w_in,
              conv_w, w_proj_conv, w_proj_attn, att_bias, w_out, norm2_w, w_up, w_down, norm_f_w):
    Bp, S = x_prompt.shape[0], x_prompt.shape[1]
    Bd = x_sample.shape[0]
    n_pages = page_table.shape[1]
    xp, xs = x_prompt, x_sample
    kp_l, vp_l, cp_l, ks_l, vs_l, cs_l = [], [], [], [], [], []
    for l in range(DEPTH):
        w = (norm1_w[l], w_in[l], conv_w[l], w_proj_conv[l], w_proj_attn[l], att_bias[l],
             w_out[l], norm2_w[l], w_up[l], w_down[l])
        conv0 = jnp.zeros((Bp, CONV_WIDTH - 1, D_CONV), xp.dtype)
        xp, cp, kp, vp = hybrid_layer(xp, conv0, None, None, *w)
        kp_l.append(kp.reshape(Bp, S // PAGE_SIZE, PAGE_SIZE, N_HEADS, HEAD_DIM))
        vp_l.append(vp.reshape(Bp, S // PAGE_SIZE, PAGE_SIZE, N_HEADS, HEAD_DIM))
        cp_l.append(cp)
        k_past = cache_k[l][page_table].reshape(Bd, n_pages * PAGE_SIZE, N_HEADS, HEAD_DIM)
        v_past = cache_v[l][page_table].reshape(Bd, n_pages * PAGE_SIZE, N_HEADS, HEAD_DIM)
        xs, cs, kn, vn = hybrid_layer(xs, state_conv[l], k_past, v_past, *w)
        ks_l.append(kn)
        vs_l.append(vn)
        cs_l.append(cs)
    y_prompt = rmsnorm(xp, norm_f_w)
    y_sample = rmsnorm(xs, norm_f_w)
    return (y_prompt, y_sample, jnp.stack(kp_l), jnp.stack(vp_l), jnp.stack(cp_l),
            jnp.stack(ks_l), jnp.stack(vs_l), jnp.stack(cs_l))


_drawn_inputs = setup_inputs


def setup_inputs(seed=0):
    import zlib

    import numpy as np

    out = dict(_drawn_inputs(seed))
    spreads = {}
    factors = {'cache_k': 5.94,
     'cache_v': 4.694,
     'w_proj_attn': 4.687,
     'att_bias': 8.0,
     'norm2_w': 3.39,
     'norm_f_w': 2.846}
    for name, (base, spread) in spreads.items():
        noise = np.random.default_rng([zlib.crc32(name.encode()), seed]).standard_normal(out[name].shape)
        drawn = base * np.exp(spread * noise) if base else spread * noise
        out[name] = __import__('jax').numpy.asarray(drawn.astype(out[name].dtype))
    for name, factor in factors.items():
        out[name] = (out[name] * factor).astype(out[name].dtype)
    return out
```

```python
from contextlib import ExitStack

import concourse.bass as bass
from concourse import mybir

F32 = mybir.dt.float32
F32R = mybir.dt.float32r
I32 = mybir.dt.int32
ALU = mybir.AluOpType
ACT = mybir.ActivationFunctionType

P = 128
EPS = 1e-6
Z_MAX = 40.0
MASKED = -1e30
Q, K, V, C, U, B = range(6)
GRAN = 4
N_CONST = 23
N_STEPS = 15
CONV_STEPS = 7


def ds(start, size):
    return bass.ds(start, size)


def hybrid_layer(nc, x_prompt, x_sample, cache_k, cache_v, state_conv, page_table, norm1_w, w_in, conv_w,
                 w_proj_conv, w_proj_attn, att_bias, w_out, norm2_w, w_up, w_down, norm_f_w,
                 y_prompt, y_sample, k_prompt, v_prompt, conv_prompt, k_sample, v_sample, conv_sample):
    _, SEQ, D = x_prompt.shape
    NSEQ, NEW, _ = x_sample.shape
    _, N_POOL, PAGE, NH, HD = cache_k.shape
    N_PAGES = page_table.shape[1]
    DC = state_conv.shape[3]
    D_FF = w_up.shape[2]
    SMP = NSEQ * NEW
    NTOK = SEQ + SMP
    KT = D // P
    NB = SEQ // P
    NPAIR = NH * HD // P
    PAST = N_PAGES * PAGE
    KEYS = PAST + SMP
    NQ = D_FF // D
    assert PAGE == P and 2 * HD == P and DC == NPAIR * P and NB == 8 and PAST == 8 * P and 2 * NEW * NSEQ == P
    CH = [(0, 364), (364, 728), (728, NTOK)]
    COL = {Q: 3 * DC, K: 3 * DC + D // 2, V: 3 * DC + D, C: DC, U: 2 * DC, B: 0}
    COL_GC, COL_GA = 3 * DC + 3 * NH * HD, 3 * DC + 3 * NH * HD + D

    xp = x_prompt.rearrange("o (a p) n -> p (o a) n", p=P)
    xs = x_sample.rearrange("b t n -> (b t) n")
    yp = y_prompt.rearrange("o (a p) n -> p (o a) n", p=P)
    ys = y_sample.rearrange("b t n -> (b t) n")
    ck = cache_k.rearrange("o n p h d -> (o n) p (h d)")
    cv = cache_v.rearrange("o n p h d -> (o n) p (h d)")
    kv_out = {K: (k_prompt.rearrange("o b a p h d -> p (o b a) (h d)"), k_sample.rearrange("o b t h d -> (o b t) (h d)")),
              V: (v_prompt.rearrange("o b a p h d -> p (o b a) (h d)"), v_sample.rearrange("o b t h d -> (o b t) (h d)"))}
    st = state_conv.rearrange("o b w c -> c (o b) w")
    cp = conv_prompt.rearrange("o b w c -> c (o b w)")
    cs = conv_sample.rearrange("o b w c -> c (o b) w")

    def rows(w):
        return w.rearrange("o (k p) n -> p (o k) n", p=P)

    win, wpc, wpa, wo, wup, wdn = map(rows, (w_in, w_proj_conv, w_proj_attn, w_out, w_up, w_down))

    ctx = ExitStack()
    with ctx:
        cursor = [(nc.sbuf_base + 31) // 32 * 32]

        def place(name, shape, dt, at=None):
            size = 4
            for n in shape[1:]:
                size *= n
            off = cursor[0] if at is None else at
            if at is None:
                cursor[0] += (size + 31) // 32 * 32
            return nc.alloc_sbuf_tensor_at(name, shape, dt, offset=off)

        ident = place("ident", [P, P], F32)
        identr = place("identr", [P, P], F32R)
        ones = place("ones", [P, P], F32)
        diag_cap = place("diag_cap", [P, P], F32)
        new_cap = place("new_cap", [P, SMP], F32)
        bias_p = place("bias_p", [P, NH], F32)
        bias_s = place("bias_s", [P, NPAIR], F32)
        w2c = place("w2c", [P, KT], F32)
        cw = place("cw", [P, NPAIR * 3], F32)
        eps = place("eps", [P, 1], F32)
        pages = place("pages", [1, NSEQ * N_PAGES], I32)
        stat = [place(f"stat{s}", [P, 4], F32) for s in range(2)]

        raw = [place(f"raw{s}", [P, KT * P], F32) for s in range(2)]
        wh = [place(f"wh{s}", [P, KT * P], F32R) for s in range(2)]
        wl = [place(f"wl{s}", [P, KT * P], F32R) for s in range(2)]

        WIDE = KT * NTOK
        r1 = cursor[0]
        xh = place("xh", [P, WIDE], F32R)
        r1b = cursor[0]
        xl = place("xl", [P, WIDE], F32R)
        mh, ml = place("mh", [P, WIDE], F32R, r1), place("ml", [P, WIDE], F32R, r1b)
        hh, hl = place("hh", [P, WIDE], F32R, r1), place("hl", [P, WIDE], F32R, r1b)
        r3 = cursor[0]
        br = place("br", [P, WIDE], F32)
        mg = place("mg", [P, WIDE], F32, r3)
        x1 = place("x1", [P, WIDE], F32, r3)
        r2 = cursor[0]
        bh, bl = place("bh", [P, WIDE], F32R), place("bl", [P, WIDE], F32R)
        yh, yl = place("yh", [P, WIDE], F32R, r2), place("yl", [P, WIDE], F32R, r2 + 4 * WIDE)
        r4 = cursor[0]
        CW = 364
        sgc, sga = place("sgc", [P, NTOK], F32), place("sga", [P, NTOK], F32)
        ssq = place("ssq", [P, NTOK], F32, r4)
        sqt = place("sqt", [P, CW], F32, r4 + 4 * NTOK)
        CWB = -(-4 * CW // 32) * 32
        XIN = r4 + 4 * NTOK + CWB
        xin = place("xin", [P, (NB + 1) * P], F32, XIN)
        tt = [place(f"tt{s}", [P, CW], F32, r4 + s * CWB) for s in range(2)]
        ts_ = [place(f"ts{s}", [P, CW], F32, r4 + (2 + s) * CWB) for s in range(2)]
        rms = place("rms", [P, NTOK], F32, r4 + 4 * CWB)
        assert max(XIN + 4 * (NB + 1) * P, r4 + 4 * CWB + 4 * NTOK) <= nc.sbuf_usable_end
        NY = 3
        yst = [place(f"yst{s}", [P, D], F32, r1 + s * 4 * D) for s in range(NY)]
        sqf = place("sqf", [P, D], F32, r1 + NY * 4 * D)
        wfb = place("wfb", [P, D], F32, r2)
        cursor[0] = r2
        qh, ql = place("qh", [P, NTOK], F32R), place("ql", [P, NTOK], F32R)
        kh, kl = place("kh", [P, NTOK], F32R), place("kl", [P, NTOK], F32R)
        vhl = place("vhl", [P, NB * 2 * P], F32R)
        NV = 2 + SEQ + NSEQ * (2 + NEW)
        vcu = place("vcu", [P, NV], F32)
        QB = P + 2 * NEW
        qblk = place("qblk", [P, NSEQ * QB], F32)
        zc = [place(f"zc{s}", [P, KEYS if s == 0 else SEQ], F32) for s in range(3)]
        sp = [place(f"sp{s}", [P, KEYS if s == 0 else SEQ], F32) for s in range(2)]
        th, tl, kct = [], [], []
        for s in range(2):
            kct.append(place(f"kct{s}", [P, 512], F32, cursor[0]))
            th.append(place(f"th{s}", [P, 512], F32R))
            tl.append(place(f"tl{s}", [P, 512], F32R))
        swT = place("swT", [P, (N_PAGES + 1) * P], F32)
        cache = [place(f"cache{s}", [P, GRAN * P], F32) for s in range(3)]
        stage = [place(f"stage{s}", [P, GRAN * P], F32) for s in range(2)]
        vnew = place("vnew", [SMP, P], F32)
        knew = place("knew", [P, SMP], F32)
        otmp = place("otmp", [P, 2 * P], F32)
        assert cursor[0] <= nc.sbuf_usable_end, cursor[0] - nc.sbuf_usable_end
        cursor[0] = r2
        xr = [place(f"xr{s}", [P, D], F32) for s in range(2)]
        sq0 = place("sq0", [P, D], F32)
        w1b = place("w1b", [P, D], F32)

        def f32(t):
            return t.bitcast(F32)

        def blocks(t, n=P):
            return t.rearrange("p (k n) -> p k n", n=n)

        ps = ctx.enter_context(nc.psum_tensor("ps", [P, 8 * 512], F32))

        def bank(b, a=0, e=512):
            return ps[:, b * 512 + a:b * 512 + e]

        DN = (0, 1)
        ZP, ZS, TURN, AVB = 2, 4, 6, 7

        credits = []

        def sem(name, credit=0):
            s = ctx.enter_context(nc.semaphore(name))
            if credit:
                credits.append((s, credit))
            return s

        consts_in = sem("consts_in")
        const_step = sem("const_step")
        consts_made = sem("consts_made")
        identr_made = sem("identr_made")
        raw_in = [sem(f"raw_in{s}") for s in range(2)]
        w_hi = sem("w_hi")
        w_split = sem("w_split", 2)
        passed = sem("passed")
        x_in = [sem(f"x_in{s}") for s in range(2)]
        x_squared, x_mean, x_root, x_rec, x_scaled = (sem(n) for n in ("x_squared", "x_mean", "x_root", "x_rec", "x_scaled"))
        x_turned = sem("x_turned", 2)
        xh_done = sem("xh_done")
        xl_done = sem("xl_done", 2)
        dense_done = sem("dense_done")
        dense_free = sem("dense_free", 2)
        evac_hi = sem("evac_hi")
        qblk_made, knew_made = sem("qblk_made"), sem("knew_made")
        turn_full = sem("turn_full")
        new_z_read = sem("new_z_read")
        turned_used = sem("turned_used", 2)
        kct_made, th_made, swt_made = sem("kct_made"), sem("th_made"), sem("swt_made")
        tl_made = sem("tl_made", 1)
        cache_in = [sem(f"cache_in{s}") for s in range(3)]
        z_full, zs_full = sem("z_full"), sem("zs_full")
        zc_ready = sem("zc_ready")
        exp_done, sp_made, suffix_made, arg_made, w_made = (sem(n) for n in ("exp_done", "sp_made", "suffix_made", "arg_made", "w_made"))
        stage_made = sem("stage_made")
        stage_out = [sem(f"stage_out{s}", 1) for s in range(2)]
        vh_made, v_made = sem("vh_made"), sem("v_made")
        otmp_made, o_made = sem("otmp_made"), sem("o_made", 1)
        sav_done = sem("sav_done", 1)
        so_copied = sem("so_copied", 1)
        so_made = sem("so_made")
        state_in = sem("state_in")
        pad_made, conv_step = sem("pad_made"), sem("conv_step")
        cu_out = sem("cu_out", 1)
        v_turned = sem("v_turned", 1)
        b_hi, b_lo = sem("b_hi"), sem("b_lo")
        gate_done, proj_done = sem("gate_done"), sem("proj_done")
        gate_free = sem("gate_free", 2)
        gated_c, gated_a = sem("gated_c"), sem("gated_a")
        m_made = sem("m_made", 3)
        m_hi, m_lo = sem("m_hi"), sem("m_lo")
        xin_in = sem("xin_in")
        xt_turned = sem("xt_turned")
        xt_free = sem("xt_free", 2)
        step_done = sem("step_done")
        step_free = sem("step_free", 6)
        y_hi, y_lo, sq_made, ssq_made = (sem(n) for n in ("y_hi", "y_lo", "sq_made", "ssq_made"))
        rms_sum, rms_root, rms_made = sem("rms_sum"), sem("rms_root"), sem("rms_made")
        s_made, h_hi, h_lo = (sem(n) for n in ("s_made", "h_hi", "h_lo"))
        wf_in = sem("wf_in")
        f_turned, f_squared, f_mean, f_root, f_rec, y_made = (sem(n) for n in ("f_turned", "f_squared", "f_mean", "f_root", "f_rec", "y_made"))
        y_out = [sem(f"y_out{s}") for s in range(NY)]

        order = []
        dense = iter([(k, c) for k in range(6) for c in range(3)])

        def dense_step():
            order.append(("dense", *next(dense)))

        for _ in range(3):
            dense_step()
        for g in range(2 * NSEQ):
            order.append(("keys", g))
            if g:
                order.append(("sample_z", g - 1))
            if g in (1, 4, 6, 9, 12, 14):
                dense_step()
        order += [("sample_z", 2 * NSEQ - 1)]
        order += [("k_out", j) for j in range(3)]
        dense_step()
        order += [("new_z",)]
        order += [("v_out", j) for j in range(3)]
        UNITS = 1 + 2 * NB

        def width(u):
            return KEYS if u == 0 else ((u - 1) % NB + 1) * P

        def groups(u):
            n = -(-width(u) // P)
            return [(a, min(a + GRAN, n)) for a in range(0, n, GRAN)]

        for n in range(UNITS + 2):
            if n < UNITS:
                order.append(("logits", n))
            if n >= 2:
                order.append(("turn", n - 2, 0))
            if n % 2 == 1 and n <= 15:
                dense_step()
            if 3 <= n < 3 + NSEQ:
                order.append(("sample_av", n - 3))
            if 1 <= n <= UNITS:
                order.append(("weights", n - 1))
            if n >= 2:
                gs = groups(n - 2)
                if n > 2:
                    order.append(("av", n - 2, 0))
                for j in range(1, len(gs)):
                    order.append(("turn", n - 2, j))
                    if n > 2:
                        order.append(("av", n - 2, j))
            if n == 3 + NSEQ:
                order.append(("sample_o",))
        assert next(dense, None) is None
        TURNS = [e for e in order if e[0] in ("keys", "new_z", "k_out", "v_out", "turn", "sample_o")]
        turn_no = {e: n for n, e in enumerate(TURNS)}
        N_TURN = len(TURNS)
        RING = [e for e in order if e[0] == "keys" or (e[0] == "turn" and e[1] > 0)]
        ring_no = {e: n for n, e in enumerate(RING)}
        N_RING = len(RING)
        W_TURNS = [e for e in order if e[0] == "turn" and e[1] > 0]
        w_no = {e: n for n, e in enumerate(W_TURNS)}
        N_W = len(W_TURNS)
        assert N_RING % 2 == 0
        N_DENSE = 18
        N_GRAN = 4 * NSEQ
        PER_SLOT = [len(range(s, N_GRAN, 3)) for s in range(3)]
        P1_DENSE = NPAIR * N_DENSE

        def apart(eng):
            eng.sem_inc(passed, 1)

        block = ctx.enter_context(nc.Block())

        @block.sync
        def _(sp_):
            def weight_tile(t, slot, views, wait):
                sp_.wait_ge(w_split, wait)
                apart(sp_)
                dst = blocks(raw[slot])
                for half, view in enumerate(views):
                    sp_.dma_start(dst[:, half * 4:half * 4 + 4, :], view).then_inc(raw_in[slot], 16)

            def halves(w, k0, col):
                return [w[:, k0 + 4 * s:k0 + 4 * s + 4, ds(col, P)] for s in range(2)]

            def row_block(it, s, b, view, n):
                sp_.wait_ge(x_turned, b + 1)
                apart(sp_)
                sp_.dma_start(xr[s][0:n, :], view).then_inc(x_in[s], 16)

            with sp_.Fori(0, NB // 2) as it:
                for s in range(2):
                    row_block(it, s, it * 2 + s, xp[:, ds(it * 2 + s, 1), :], P)
            row_block(None, 0, NB, xs, SMP)

            def cache_granule(i, gi):
                slot, m = gi % 3, gi // 3
                src = ck if gi < 2 * NSEQ else cv
                if gi >= 3:
                    old = gi - 3
                    if old < 2 * NSEQ:
                        sp_.wait_ge(turn_full, i * N_TURN + turn_no[("keys", old)] + 1)
                    else:
                        sp_.wait_ge(sav_done, i * NSEQ + (old - 2 * NSEQ) // 2 + 1 + 1)
                else:
                    sp_.wait_ge(sav_done, i * NSEQ + 1)
                apart(sp_)
                at = (gi % (2 * NSEQ)) * GRAN
                numbers = [sp_.value_load(pages[0:1, at + j:at + j + 1]) for j in range(GRAN)]
                for j, page in enumerate(numbers):
                    sp_.dma_start(cache[slot][:, j * P:(j + 1) * P].rearrange("p (o n) -> p o n", o=1),
                                  src[ds(page, 1), :, ds(i * P, P)].rearrange("o p n -> p o n")).then_inc(cache_in[slot], 16)

            def store_rows(i, tile, j):
                s = (3 * (tile == V) + j) % 2
                sp_.wait_ge(stage_made, i * 6 + 3 * (tile == V) + j + 1)
                apart(sp_)
                prompt, sample = kv_out[tile]
                if j < 2:
                    sp_.dma_start(prompt[:, j * GRAN:(j + 1) * GRAN, ds(i * P, P)], blocks(stage[s])).then_inc(stage_out[s], 16)
                else:
                    sp_.dma_start(sample[:, ds(i * P, P)], stage[s][0:SMP, 0:P]).then_inc(stage_out[s], 16)

            sp_.wait_ge(consts_in, 16 * N_CONST)
            with sp_.Fori(0, NPAIR) as i:
                for k in (Q, K):
                    weight_tile(None, k % 2, halves(win, 0, i * P + COL[k]), i * 6 + k + 1)
                done = 0
                for gi in range(3):
                    cache_granule(i, gi)
                done = 3
                for e in order:
                    if e[0] == "dense" and e[2] == 0 and e[1] < 4:
                        k = e[1] + 2
                        weight_tile(None, k % 2, halves(win, 0, i * P + COL[k]), i * 6 + k + 1)
                    if e[0] == "keys" and done < 2 * NSEQ + 3 and e[1] >= 1:
                        cache_granule(i, done)
                        done += 1
                    if e[0] == "sample_av":
                        for _ in range(2):
                            if done < N_GRAN:
                                cache_granule(i, done)
                                done += 1
                    if e[0] == "sample_z" and e[1] == 2 * NSEQ - 1:
                        while done < 2 * NSEQ + 3:
                            cache_granule(i, done)
                            done += 1
                    if e[0] == "k_out":
                        store_rows(i, K, e[1])
                    if e[0] == "v_out":
                        store_rows(i, V, e[1])
                        if e[1] == 2:
                            sp_.wait_ge(turn_full, i * N_TURN + turn_no[("v_out", 2)] + 1)
                            apart(sp_)
                            with nc.allow_non_contiguous_dma(reason="two columns per sequence"):
                                for b in range(NSEQ):
                                    a = 2 + SEQ + b * (2 + NEW)
                                    sp_.dma_start(vcu[:, a:a + 2].rearrange("p (o w) -> p o w", o=1),
                                                  st[ds(i * P, P), b:b + 1, :]).then_inc(state_in, 16)
                sp_.wait_ge(dense_free, i * N_DENSE + 3 * U + 3 + 2)
                apart(sp_)
                with nc.allow_non_contiguous_dma(reason="two rows per sequence"):
                    sp_.dma_start(cp[ds(i * P, P), :], vcu[:, SEQ:SEQ + 2]).then_inc(cu_out, 16)
                    for b in range(NSEQ):
                        a = 2 + SEQ + b * (2 + NEW) + NEW
                        sp_.dma_start(cs[ds(i * P, P), b:b + 1, :],
                                      vcu[:, a:a + 2].rearrange("p (o w) -> p o w", o=1)).then_inc(cu_out, 16)

            base = 6 * NPAIR
            with sp_.Fori(0, KT // 2) as j:
                for h in range(2):
                    f = j * 2 + h
                    for k, views in enumerate((halves(win, 0, f * P + COL_GC), halves(win, 0, f * P + COL_GA),
                                               [wpc[:, 0:4, ds(f * P, P)], wpa[:, 0:4, ds(f * P, P)]])):
                        weight_tile(None, (3 * h + k) % 2, views, j * 6 + base + 3 * h + k + 1)
            base += 3 * KT
            with sp_.Fori(0, KT // 2) as j:
                for h in range(2):
                    f = j * 2 + h
                    weight_tile(None, h, halves(wo, 0, f * P), j * 2 + base + h + 1)
                    if h == 0:
                        sp_.wait_ge(m_made, 3 * KT + 3)
                    sp_.wait_ge(xt_free, j * 6 + 3 * h + 2)
                    apart(sp_)
                    sp_.dma_start(blocks(xin)[:, 0:NB, :], xp[:, :, ds(f * P, P)]).then_inc(xin_in, 16)
                    sp_.dma_start(xin[0:SMP, NB * P:], xs[:, ds(f * P, P)]).then_inc(xin_in, 16)
            base += KT
            with sp_.Fori(0, NQ) as g:
                with sp_.Fori(0, KT // 2) as j:
                    for h in range(2):
                        weight_tile(None, h, halves(wup, 0, g * D + j * (2 * P) + h * P), g * (2 * KT) + j * 2 + base + h + 1)
                with sp_.Fori(0, KT // 2) as j:
                    for h in range(2):
                        col = j * (2 * P) + h * P
                        weight_tile(None, h, [wdn[:, ds(g * KT + 4 * s, 4), ds(col, P)] for s in range(2)],
                                    g * (2 * KT) + j * 2 + base + KT + h + 1)
            sp_.wait_ge(step_done, 3 * (KT + 2 * KT * NQ))
            sp_.dma_start(wfb[:, :], norm_f_w.rearrange("(o n) -> o n", o=1).to_broadcast([P, D])).then_inc(wf_in, 16)
            for b in range(NB + 1):
                s = b % NY
                n = P if b < NB else SMP
                sp_.wait_ge(y_made, b + 1)
                sp_.dma_start(yp[:, b, :] if b < NB else ys, yst[s][0:n, :]).then_inc(y_out[s], 16)
            for s in range(NY):
                sp_.wait_ge(y_out[s], 16 * len(range(s, NB + 1, NY)))
            for s in range(2):
                sp_.wait_ge(stage_out[s], 16 * 3 * NPAIR + 1)
            sp_.wait_ge(cu_out, 16 * (1 + NSEQ) * NPAIR + 1)

        @block.gpsimd
        def _(pool):
            g = nc.gpsimd
            for s, n in credits:
                pool.sem_inc(s, n)
            steps = [0]

            def step(ins):
                steps[0] += 1
                ins.then_inc(const_step, 1)
                pool.wait_ge(const_step, steps[0])

            step(g.memset(ident[:, :], 1.0))
            step(g.affine_select(out=ident[:, :], in_=ident[:, :], compare_op=ALU.is_equal, fill=0.0, base=0,
                                 pattern=[[-1, P]], channel_multiplier=1))
            step(g.memset(diag_cap[:, :], Z_MAX))
            step(g.affine_select(out=diag_cap[:, :], in_=diag_cap[:, :], compare_op=ALU.is_gt, fill=MASKED, base=0,
                                 pattern=[[-1, P]], channel_multiplier=1))
            for h, cap in ((0, new_cap[:, :]), (1, ones[:, 0:SMP])):
                step(g.memset(cap, 0.0))
                v = cap.rearrange("p (b t) -> p b t", t=NEW)
                step(g.affine_select(out=v, in_=v, compare_op=ALU.is_gt, fill=1.0, base=-NEW * h,
                                     pattern=[[-2 * NEW, NSEQ], [-1, NEW]], channel_multiplier=1))
                step(g.affine_select(out=v, in_=v, compare_op=ALU.is_ge, fill=1.0, base=NEW - 1 + NEW * h,
                                     pattern=[[2 * NEW, NSEQ], [0, NEW]], channel_multiplier=-1))
            step(g.tensor_tensor(new_cap[:, :], new_cap[:, :], ones[:, 0:SMP], ALU.mult))
            step(g.tensor_scalar(new_cap[:, :], new_cap[:, :], MASKED, Z_MAX, ALU.mult, ALU.add))
            step(g.memset(ones[:, :], 1.0))
            step(g.memset(eps[:, :], EPS))
            step(g.memset(qblk[:, :], 0.0))
            pool.sem_inc(consts_made, 1)

            def split(t2, s, used):
                pool.wait_ge(raw_in[s], t2 * 32 + 32)
                if used is not None:
                    pool.wait_ge(*used)
                apart(pool)
                g.tensor_copy(wh[s][:, :], raw[s][:, :]).then_inc(w_hi, 1)
                return s

            def split_lo(s, t):
                pool.wait_ge(w_hi, t + 1)
                apart(pool)
                g.tensor_tensor(wl[s][:, :], raw[s][:, :], f32(wh[s][:, :]), ALU.subtract).then_inc(w_split, 1)

            for t in range(2):
                split(0, t, None)
                split_lo(t, t)
            with g.Fori(1, 3 * NPAIR) as j:
                for s in range(2):
                    split(j, s, (dense_done, j * 6 + 3 * s - 6 + 3))
                    split_lo(s, j * 2 + s)
            T0 = 3 * NPAIR
            for t in range(2):
                split(T0, t, (dense_done, P1_DENSE - 3 + 3 * t))
                split_lo(t, 2 * T0 + t)

            def p2_tile(j, n, used):
                split(j * 3 + (T0 + n // 2), n % 2, used)
                split_lo(n % 2, j * 6 + (2 * T0 + n))

            def p2_rest(j):
                p2_tile(j, 2, (gate_done, j * 12 + 3))
                p2_tile(j, 3, (gate_done, j * 12 + 6))
                p2_tile(j, 4, (proj_done, j * 6 + 3))
                p2_tile(j, 5, (gate_done, j * 12 + 9))
            p2_rest(0)
            with g.Fori(1, KT // 2) as j:
                p2_tile(j, 0, (gate_done, j * 12))
                p2_tile(j, 1, (proj_done, j * 6))
                p2_rest(j)
            T1 = T0 + 3 * KT // 2
            split(T1, 0, (gate_done, 6 * KT))
            split_lo(0, 2 * T1)
            split(T1, 1, (proj_done, 3 * KT))
            split_lo(1, 2 * T1 + 1)
            with g.Fori(1, (KT + 2 * KT * NQ) // 2) as j:
                for s in range(2):
                    split(j + T1, s, (step_done, j * 6 + 3 * s - 6 + 3))
                    split_lo(s, j * 2 + (2 * T1 + s))

        @block.tensor
        def _(pe):
            mm, tr = nc.tensor.matmul, nc.tensor.transpose

            def product(out, w, lo_w, ks, mov_h, mov_l, cols):
                n = len(ks)
                for a, k in enumerate(ks):
                    x = slice(k * NTOK + cols[0], k * NTOK + cols[1])
                    for m, (lhs, rhs) in enumerate(((w, mov_h), (w, mov_l), (lo_w, mov_h))):
                        ins = mm(out, lhs[:, k * P:(k + 1) * P], rhs[:, x], start=(a == 0 and m == 0),
                                 stop=(a == n - 1 and m == 2))
                return ins

            def width_of(c):
                return CH[c][1] - CH[c][0]

            def turn_rows(s, b, n):
                pe.wait_ge(x_scaled, b + 1)
                pe.wait_ge(xl_done, b + 1)
                for f in range(KT):
                    ins = tr(ps[:, s * 1024 + f * P:s * 1024 + f * P + n], xr[s][0:n, f * P:(f + 1) * P], ident[0:n, 0:n])
                ins.then_inc(x_turned, 1)

            pe.wait_ge(consts_made, 1)
            pe.wait_ge(const_step, N_STEPS)
            with pe.Fori(0, NB // 2) as it:
                for s in range(2):
                    turn_rows(s, it * 2 + s, P)
            turn_rows(0, NB, SMP)
            pe.wait_ge(xl_done, NB + 1 + 2)
            pe.wait_ge(identr_made, 1)

            def p1(i):
                def turn_wait(e):
                    last = TURNS[turn_no[e] - 1]
                    if turn_no[e] == 0:
                        pe.wait_ge(tl_made, i * N_W + 1)
                    elif last[0] == "keys":
                        pe.wait_ge(kct_made, i * (2 * NSEQ) + last[1] + 1)
                    elif last[0] == "new_z":
                        pe.wait_ge(new_z_read, i + 1)
                    elif last[0] in ("k_out", "v_out"):
                        pe.wait_ge(stage_made, i * 6 + 3 * (last[0] == "v_out") + last[1] + 1)
                    elif last[0] == "sample_o":
                        pe.wait_ge(so_made, i + 1)
                    elif last[1] == 0:
                        pe.wait_ge(swt_made, i * 3 + last[2] + 1)
                    else:
                        pe.wait_ge(tl_made, i * N_W + w_no[last] + 1 + 1)

                for e in order:
                    if e[0] == "dense":
                        _, k, c = e
                        d = 3 * k + c
                        pe.wait_ge(w_split, i * 6 + k + 1 + 2)
                        pe.wait_ge(dense_free, i * N_DENSE + d + 1)
                        product(bank(DN[d % 2], 0, width_of(c)), wh[k % 2], wl[k % 2], range(KT), xh, xl, CH[c]).then_inc(dense_done, 1)
                    elif e[0] == "keys":
                        turn_wait(e)
                        s = e[1] % 3
                        pe.wait_ge(cache_in[s], i * (64 * PER_SLOT[s]) + 64 * (e[1] // 3 + 1))
                        for j in range(GRAN):
                            ins = tr(bank(TURN, j * P, (j + 1) * P), cache[s][:, j * P:(j + 1) * P], ident[:, :])
                        ins.then_inc(turn_full, 1)
                    elif e[0] == "sample_z":
                        g = e[1]
                        b, half = g // 2, g % 2
                        s = ring_no[("keys", g)] % 2
                        if g == 0:
                            pe.wait_ge(qblk_made, i * 2 + 2)
                            pe.wait_ge(so_copied, i + 1)
                        pe.wait_ge(kct_made, i * (2 * NSEQ) + g + 1)
                        at = b * QB - b * 2 * NEW
                        ins = mm(bank(ZS + half), qblk[:, at:at + P], kct[s][:, :], start=(b == 0), stop=(b == NSEQ - 1))
                        ins.then_inc(turned_used, 1)
                    elif e[0] == "new_z":
                        turn_wait(e)
                        pe.wait_ge(knew_made, i + 1)
                        for b in range(NSEQ):
                            at = b * QB - b * 2 * NEW
                            ins = mm(bank(TURN, 0, SMP), qblk[:, at:at + P], knew[:, :], start=(b == 0), stop=(b == NSEQ - 1))
                        ins.then_inc(turn_full, 1)
                    elif e[0] == "k_out":
                        turn_wait(e)
                        pe.wait_ge(dense_free, i * N_DENSE + 3 * K + 3 + 2)
                        for b in range(GRAN * e[1], min(GRAN * e[1] + GRAN, NB + 1)):
                            n = P if b < NB else SMP
                            out = ps[0:n, TURN * 512 + (b % GRAN) * P:TURN * 512 + (b % GRAN) * P + P]
                            mm(out, kh[:, b * P:b * P + n], identr[:, :], start=True, stop=False)
                            ins = mm(out, kl[:, b * P:b * P + n], identr[:, :], start=False, stop=True)
                        ins.then_inc(turn_full, 1)
                    elif e[0] == "v_out":
                        turn_wait(e)
                        pe.wait_ge(dense_free, i * N_DENSE + 3 * V + 3 + 2)
                        apart(pe)
                        for b in range(GRAN * e[1], min(GRAN * e[1] + GRAN, NB + 1)):
                            n = P if b < NB else SMP
                            ins = tr(ps[0:n, TURN * 512 + (b % GRAN) * P:TURN * 512 + (b % GRAN) * P + P],
                                     vcu[:, b * P:b * P + n], ident[:, :])
                        ins.then_inc(turn_full, 1)
                    elif e[0] == "logits":
                        u = e[1]
                        if u == 0:
                            continue
                        h, t = (u - 1) // NB, (u - 1) % NB
                        r = slice(h * HD, h * HD + HD)
                        pe.wait_ge(zc_ready, i * UNITS + u)
                        for a in range(0, width(u), 512):
                            z = min(width(u), a + 512)
                            for m, (x, y) in enumerate(((qh, kh), (qh, kl), (ql, kh))):
                                ins = mm(ps[:, ZP * 512 + a:ZP * 512 + z], x[r, t * P:(t + 1) * P], y[r, a:z],
                                         start=(m == 0), stop=(m == 2))
                        ins.then_inc(z_full, 1)
                    elif e[0] == "turn":
                        u, (a, z) = e[1], groups(e[1])[e[2]]
                        turn_wait(e)
                        if e[2] == 0:
                            pe.wait_ge(w_made, i * UNITS + u + 1)
                        if u == 0:
                            apart(pe)
                        for j in range(a, z):
                            n = min(P, width(u) - j * P)
                            ins = tr(ps[0:n, TURN * 512 + (j - a) * P:TURN * 512 + (j - a) * P + P],
                                     zc[u % 3][:, j * P:j * P + n], ident[:, :])
                        ins.then_inc(turn_full, 1)
                    elif e[0] == "av":
                        u, (a, z) = e[1], groups(e[1])[e[2]]
                        h, t = (u - 1) // NB, (u - 1) % NB
                        key = ("turn", u, e[2])
                        s = ring_no[key] % 2
                        if e[2] == 0 and t % 2 == 0:
                            pe.wait_ge(o_made, i * NB + h * (NB // 2) + t // 2 + 1)
                        pe.wait_ge(tl_made, i * N_W + w_no[key] + 1 + 1)
                        if u == 1:
                            pe.wait_ge(v_made, i * 3 + 3)
                        out = bank(AVB, (t % 2) * P, (t % 2) * P + P)
                        for j in range(a, z):
                            v = vhl[:, (j * 2 + h) * P:(j * 2 + h + 1) * P]
                            mm(out, v, th[s][:, (j - a) * P:(j - a + 1) * P], start=(j == 0), stop=False)
                            ins = mm(out, v, tl[s][:, (j - a) * P:(j - a + 1) * P], start=False, stop=(j == t))
                        ins.then_inc(turned_used, 1)
                    elif e[0] == "sample_av":
                        b = e[1]
                        if b == 0:
                            pe.wait_ge(swt_made, i * 3 + 3)
                            pe.wait_ge(v_made, i * 3 + 3)
                        out = ps[0:2 * NEW, ZS * 512 + b * P:ZS * 512 + (b + 1) * P]
                        for half in range(2):
                            gi = 2 * NSEQ + 2 * b + half
                            s = gi % 3
                            pe.wait_ge(cache_in[s], i * (64 * PER_SLOT[s]) + 64 * (gi // 3 + 1))
                            for j in range(GRAN):
                                at = (half * GRAN + j) * P + b * 2 * NEW
                                mm(out, swT[:, at:at + 2 * NEW], cache[s][:, j * P:(j + 1) * P],
                                   start=(half == 0 and j == 0), stop=False)
                        at = N_PAGES * P + b * 2 * NEW
                        mm(out, swT[0:SMP, at:at + 2 * NEW], vnew[:, :], start=False, stop=True,
                           ).then_inc(sav_done, 1)
                    elif e[0] == "sample_o":
                        turn_wait(e)
                        pe.wait_ge(so_copied, i + 1 + 1)
                        apart(pe)
                        for b in range(NSEQ):
                            ins = tr(bank(TURN, b * 2 * NEW, (b + 1) * 2 * NEW), swT[0:2 * NEW, b * P:(b + 1) * P],
                                     ident[0:2 * NEW, 0:2 * NEW])
                        ins.then_inc(turn_full, 1)

            with pe.Fori(0, NPAIR) as i:
                p1(i)

            pe.wait_ge(dense_free, P1_DENSE + 2)
            pe.wait_ge(so_made, NPAIR)
            pe.wait_ge(o_made, NPAIR * NB + 1)
            base = 6 * NPAIR + 2
            with pe.Fori(0, KT // 2) as j:
                for h in range(2):
                    for k in range(2):
                        n = 3 * h + k
                        pe.wait_ge(w_split, j * 6 + base + n + 1)
                        for c in range(3):
                            d = 6 * h + 3 * k + c
                            pe.wait_ge(gate_free, j * 12 + d + 1)
                            product(bank(d % 2, 0, width_of(c)), wh[n % 2], wl[n % 2], range(KT), xh, xl, CH[c]).then_inc(gate_done, 1)
                    n = 3 * h + 2
                    pe.wait_ge(w_split, j * 6 + base + n + 1)
                    pe.wait_ge(b_lo, 8)
                    for c in range(3):
                        d = 3 * h + c
                        pe.wait_ge(m_made, j * 6 + d + 1 + 1)
                        product(bank(2 + 2 * (d % 2), 0, width_of(c)), wh[n % 2], wl[n % 2], range(4), bh, bl, CH[c])
                        product(bank(3 + 2 * (d % 2), 0, width_of(c)), wh[n % 2], wl[n % 2], range(4, KT), bh, bl, CH[c]).then_inc(proj_done, 1)

            pe.wait_ge(gate_free, 6 * KT + 2)
            pe.wait_ge(m_made, 3 * KT + 3)
            base = 6 * NPAIR + 3 * KT + 2

            def plain_tile(slot, tile_no, first_step, mov_h, mov_l, ready=None):
                pe.wait_ge(w_split, tile_no)
                for c in range(3):
                    pe.wait_ge(step_free, first_step + c + 1)
                    if ready is not None:
                        pe.wait_ge(ready[0], ready[1] + c)
                    product(bank(3 * slot + c, 0, width_of(c)), wh[slot], wl[slot], range(KT), mov_h, mov_l, CH[c]).then_inc(step_done, 1)

            with pe.Fori(0, KT // 2) as j:
                for h in range(2):
                    pe.wait_ge(xin_in, j * 64 + h * 32 + 32)
                    for g in range(3):
                        n = 3 * h + g
                        pe.wait_ge(xt_free, j * 6 + n + 1)
                        apart(pe)
                        for b in range(GRAN * g, min(GRAN * g + GRAN, NB + 1)):
                            m = P if b < NB else SMP
                            ins = tr(bank(6 + n % 2, (b % GRAN) * P, (b % GRAN) * P + m), xin[0:m, b * P:(b + 1) * P], ident[0:m, 0:m])
                        ins.then_inc(xt_turned, 1)
                    plain_tile(h, j * 2 + base + h + 1, j * 6 + 3 * h, mh, ml, (m_lo, 1))
            for c in range(3):
                pe.wait_ge(ssq_made, 3 * KT - 1 + c)
                if c == 0:
                    pe.wait_ge(xt_free, 3 * KT + 2)
                if c == 2:
                    pe.wait_ge(rms_root, 1)
                mm(bank(6 + c % 2, 0, width_of(c)), ones[:, :], ssq[:, CH[c][0]:CH[c][1]], start=True, stop=True).then_inc(rms_sum, 1)
            base += KT
            with pe.Fori(0, NQ) as g:
                with pe.Fori(0, KT // 2) as j:
                    for s in range(2):
                        plain_tile(s, g * (2 * KT) + j * 2 + base + s + 1, g * (6 * KT) + j * 6 + 3 * KT + 3 * s, yh, yl, (y_lo, 3 * KT - 2))
                with pe.Fori(0, KT // 2) as j:
                    for s in range(2):
                        plain_tile(s, g * (2 * KT) + j * 2 + base + KT + s + 1, g * (6 * KT) + j * 6 + 6 * KT + 3 * s, hh, hl,
                                   (h_lo, g * (3 * KT) + 3 * KT - 2))
            for b in range(NB + 1):
                n = P if b < NB else SMP
                if b == 0:
                    pe.wait_ge(step_free, 3 * (KT + 2 * KT * NQ) + 6)
                    pe.wait_ge(rms_made, 3)
                if b >= 4:
                    pe.wait_ge(y_made, b - 3)
                for f in range(KT):
                    at = (b % 4) * 1024 + f * P
                    ins = tr(ps[0:n, at:at + P], x1[:, f * NTOK + b * P:f * NTOK + b * P + n], ident[:, :])
                ins.then_inc(f_turned, 1)

        @block.scalar
        def _(act):
            A = nc.scalar.activation
            with nc.allow_non_contiguous_dma(reason="small constants"):
                act.dma_start(w1b[:, :], norm1_w.to_broadcast([P, D])).then_inc(consts_in, 16)
                act.dma_start(pages[:, :], page_table.rearrange("b n -> (b n)").rearrange("(o n) -> o n", o=1)).then_inc(consts_in, 16)
                act.dma_start(bias_p[:, :], att_bias.to_broadcast([P, NH])).then_inc(consts_in, 16)
                for b in range(NSEQ):
                    for h in range(2):
                        r = 2 * NEW * b + NEW * h
                        act.dma_start(bias_s[r:r + NEW, :].rearrange("p (n o) -> p n o", o=1),
                                      att_bias.rearrange("o (n h) -> o n h", h=2)[:, :, h:h + 1].to_broadcast([NEW, NPAIR, 1])).then_inc(consts_in, 16)
                act.dma_start(w2c[:, :], norm2_w.rearrange("o (k p) -> p (o k)", p=P)).then_inc(consts_in, 16)
                for w in range(3):
                    act.dma_start(cw[:, :].rearrange("p (n w) -> p n w", w=3)[:, :, w:w + 1],
                                  conv_w[:, w:w + 1, :].rearrange("o w (n p) -> p n (o w)", p=P)).then_inc(consts_in, 16)

            def root(s, b, n):
                act.wait_ge(x_mean, b + 1)
                A(stat[s][0:n, 2:3], stat[s][0:n, 1:2], ACT.Sqrt).then_inc(x_root, 1)

            def x_hi(s, b, n, cols):
                act.wait_ge(x_turned, b + 1 + 2)
                apart(act)
                A(blocks(xh, NTOK)[:, :, cols], blocks(ps[:, s * 1024:(s + 1) * 1024])[:, :, 0:n], ACT.Copy).then_inc(xh_done, 1)

            with act.Fori(0, NB // 2) as it:
                for s in range(2):
                    act.wait_ge(x_in[s], it * 16 + 16)
                    act.wait_ge(x_turned, it * 2 + s + 1)
                    if s == 1:
                        act.wait_ge(x_squared, it * 2 + 1)
                    A(sq0[:, :], xr[s][:, :], ACT.Square, accum_out=stat[s][:, 0:1]).then_inc(x_squared, 1)
                for s in range(2):
                    root(s, it * 2 + s, P)
                for s in range(2):
                    x_hi(s, it * 2 + s, P, ds((it * 2 + s) * P, P))
            act.wait_ge(x_in[0], (NB // 2) * 16 + 16)
            act.wait_ge(x_turned, NB + 1)
            act.wait_ge(x_squared, NB)
            A(sq0[0:SMP, :], xr[0][0:SMP, :], ACT.Square, accum_out=stat[0][0:SMP, 0:1]).then_inc(x_squared, 1)
            root(0, NB, SMP)
            x_hi(0, NB, SMP, slice(SEQ, NTOK))

            def evac(i, d):
                k, c = d // 3, d % 3
                if k in (Q, K):
                    act.wait_ge(dense_done, i * N_DENSE + d + 1)
                    dst = (qh, kh)[k]
                    A(dst[:, CH[c][0]:CH[c][1]], bank(DN[d % 2], 0, CH[c][1] - CH[c][0]), ACT.Copy,
                      scale=HD ** -0.5 if k == Q else 1.0).then_inc(evac_hi, 1)

            def p1(i):
                def turned(e):
                    act.wait_ge(turn_full, i * N_TURN + turn_no[e] + 1)

                for e in order:
                    if e[0] == "dense":
                        if 3 * e[1] + e[2] > 0:
                            evac(i, 3 * e[1] + e[2] - 1)
                    elif e[0] == "keys":
                        s = ring_no[e] % 2
                        turned(e)
                        act.wait_ge(turned_used, i * N_RING + ring_no[e] + 1)
                        A(kct[s][:, :], bank(TURN), ACT.Copy).then_inc(kct_made, 1)
                    elif e[0] in ("k_out", "v_out"):
                        m = 3 * (e[0] == "v_out") + e[1]
                        s = m % 2
                        turned(e)
                        act.wait_ge(stage_out[s], i * 48 + 16 * (m // 2) + 1)
                        if m >= 5:
                            act.wait_ge(v_made, i * 3 + m - 4)
                        n, w = (P, 512) if e[1] < 2 else (SMP, P)
                        A(stage[s][0:n, 0:w], ps[0:n, TURN * 512:TURN * 512 + w], ACT.Copy).then_inc(stage_made, 1)
                    elif e[0] == "logits":
                        u = e[1]
                        act.wait_ge(zc_ready, i * UNITS + u + 1)
                        A(sp[u % 2][:, 0:width(u)], zc[u % 3][:, 0:width(u)], ACT.Exp).then_inc(exp_done, 1)
                        act.wait_ge(exp_done, i * UNITS + u + 1)
                        A(sp[u % 2][:, 0:width(u)], sp[u % 2][:, 0:width(u)], ACT.Ln, bias=1.0).then_inc(sp_made, 1)
                    elif e[0] == "weights":
                        u = e[1]
                        act.wait_ge(arg_made, i * UNITS + u + 1)
                        A(zc[u % 3][:, 0:width(u)], zc[u % 3][:, 0:width(u)], ACT.Exp).then_inc(w_made, 1)
                    elif e[0] == "turn":
                        u, (a, z) = e[1], groups(e[1])[e[2]]
                        turned(e)
                        if u == 0:
                            n = min(P, width(0) - a * P)
                            A(swT[0:n, a * P:z * P], ps[0:n, TURN * 512:TURN * 512 + (z - a) * P], ACT.Copy).then_inc(swt_made, 1)
                        else:
                            act.wait_ge(turned_used, i * N_RING + ring_no[e] + 1)
                            A(th[ring_no[e] % 2][:, 0:(z - a) * P], bank(TURN, 0, (z - a) * P), ACT.Copy).then_inc(th_made, 1)
                    elif e[0] == "av":
                        u, (a, z) = e[1], groups(e[1])[e[2]]
                        h, t = (u - 1) // NB, (u - 1) % NB
                        if z == t + 1 and t % 2 == 1:
                            m = h * (NB // 2) + t // 2
                            act.wait_ge(turned_used, i * N_RING + ring_no[("turn", u, e[2])] + 1 + 2)
                            act.wait_ge(o_made, i * NB + m + 1)
                            r, o = slice(h * HD, h * HD + HD), slice(HD - h * HD, 2 * HD - h * HD)
                            A(otmp[r, :], ps[o, AVB * 512:AVB * 512 + 2 * P], ACT.Copy).then_inc(otmp_made, 1)
                    elif e[0] == "sample_av" and e[1] == NSEQ - 1:
                        act.wait_ge(sav_done, i * NSEQ + NSEQ + 1)
                        A(swT[0:2 * NEW, 0:NSEQ * P], ps[0:2 * NEW, ZS * 512:ZS * 512 + NSEQ * P], ACT.Copy).then_inc(so_copied, 1)

            act.preload_act_table_set("natural_log_exp_and_others")
            with act.Fori(0, NPAIR) as i:
                p1(i)

            act.wait_ge(so_made, NPAIR)
            act.wait_ge(o_made, NPAIR * NB + 1)
            act.wait_ge(dense_free, P1_DENSE + 2)
            for s in range(2):
                act.wait_ge(stage_out[s], 48 * NPAIR + 1)
            act.wait_ge(cu_out, 16 * (1 + NSEQ) * NPAIR + 1)
            for k in range(KT):
                A(bh[:, k * NTOK:(k + 1) * NTOK], br[:, k * NTOK:(k + 1) * NTOK], ACT.Copy).then_inc(b_hi, 1)
            with act.Fori(0, KT // 2) as j:
                for h in range(2):
                    for k in range(2):
                        for c in range(3):
                            d = 6 * h + 3 * k + c
                            act.wait_ge(gate_done, j * 12 + d + 1)
                            act.wait_ge(m_made, j * 6 + 3 * h + c + 1)
                            A((sgc, sga)[k][:, CH[c][0]:CH[c][1]], bank(d % 2, 0, CH[c][1] - CH[c][0]), ACT.Sigmoid).then_inc(gate_free, 1)
            act.wait_ge(gate_done, 6 * KT)
            for c in range(3):
                act.wait_ge(m_made, 3 * KT - 3 + c + 1 + 3)
                A(blocks(mh, NTOK)[:, :, CH[c][0]:CH[c][1]], blocks(mg, NTOK)[:, :, CH[c][0]:CH[c][1]], ACT.Copy).then_inc(m_hi, 1)
            act.wait_ge(m_lo, 3)

            with act.Fori(0, KT // 2) as j:
                for h in range(2):
                    f = j * 2 + h
                    for g in range(3):
                        n = 3 * h + g
                        w = 512 if g < 2 else SMP
                        act.wait_ge(xt_turned, j * 6 + n + 1)
                        apart(act)
                        A(x1[:, ds(f * NTOK + g * 512, w)], bank(6 + n % 2, 0, w), ACT.Copy).then_inc(xt_free, 1)
                    for c in range(3):
                        n, (a, z) = 3 * h + c, CH[c]
                        act.wait_ge(step_free, j * 6 + n + 1 + 6)
                        apart(act)
                        A(yh[:, ds(f * NTOK + a, z - a)], x1[:, ds(f * NTOK + a, z - a)], ACT.Copy, scale=w2c[:, ds(f, 1)]).then_inc(y_hi, 1)
                        act.wait_ge(ssq_made, j * 6 + n + 1)
                        apart(act)
                        A(sqt[:, 0:z - a], x1[:, ds(f * NTOK + a, z - a)], ACT.Square).then_inc(sq_made, 1)
            for c in range(3):
                a, z = CH[c]
                act.wait_ge(rms_sum, c + 1)
                if c == 0:
                    act.wait_ge(xt_turned, 3 * KT)
                A(rms[:, a:z], bank(6 + c % 2, 0, z - a), ACT.Sqrt, scale=1.0 / D, bias=eps[:, 0:1]).then_inc(rms_root, 1)
            with act.Fori(0, NQ) as g:
                with act.Fori(0, KT // 2) as j:
                    for n in range(6):
                        s, (a, z) = n % 2, CH[n % 3]
                        no = g * (3 * KT) + j * 6
                        act.wait_ge(step_free, g * (6 * KT) + j * 6 + 3 * KT + n + 1 + 6)
                        A(ts_[s][:, 0:z - a], tt[s][:, 0:z - a], ACT.Square).then_inc(s_made, 1)
                        act.wait_ge(s_made, no + n + 1)
                        apart(act)
                        A(hh[:, ds((j * 2 + n // 3) * NTOK + a, z - a)], ts_[s][:, 0:z - a], ACT.Copy).then_inc(h_hi, 1)
            for b in range(NB + 1):
                n, s = (P if b < NB else SMP), b % 2
                act.wait_ge(f_turned, b + 1)
                if b >= 1:
                    act.wait_ge(f_squared, b)
                if b >= 2:
                    act.wait_ge(y_made, b - 1)
                A(sqf[0:n, :], ps[0:n, (b % 4) * 1024:(b % 4) * 1024 + D], ACT.Square, accum_out=stat[s][0:n, 0:1]).then_inc(f_squared, 1)
                act.wait_ge(f_mean, b + 1)
                A(stat[s][0:n, 2:3], stat[s][0:n, 1:2], ACT.Sqrt).then_inc(f_root, 1)

        @block.vector
        def _(v):
            V_ = nc.vector
            v.wait_ge(const_step, N_STEPS)
            V_.tensor_copy(identr[:, :], ident[:, :]).then_inc(identr_made, 1)

            v.wait_ge(consts_in, 16 * N_CONST)

            def scale_rows(s, b, n, first):
                r = stat[s]
                v.wait_ge(x_squared, b + 1)
                V_.tensor_scalar(r[0:n, 1:2], r[0:n, 0:1], 1.0 / D, EPS, ALU.mult, ALU.add).then_inc(x_mean, 1)

            def normalise(s, b, n):
                r = stat[s]
                v.wait_ge(x_root, b + 1)
                V_.reciprocal(r[0:n, 3:4], r[0:n, 2:3]).then_inc(x_rec, 1)
                v.wait_ge(x_rec, b + 1)
                V_.scalar_tensor_tensor(out=xr[s][0:n, :], in0=xr[s][0:n, :], scalar=r[0:n, 3:4], in1=w1b[0:n, :],
                                        op0=ALU.mult, op1=ALU.mult).then_inc(x_scaled, 1)

            def x_lo(s, b, n, cols):
                v.wait_ge(xh_done, b + 1)
                V_.tensor_tensor(blocks(xl, NTOK)[:, :, cols], blocks(ps[:, s * 1024:(s + 1) * 1024])[:, :, 0:n],
                                 f32(blocks(xh, NTOK)[:, :, cols]), ALU.subtract).then_inc(xl_done, 1)

            with v.Fori(0, NB // 2) as it:
                for s in range(2):
                    scale_rows(s, it * 2 + s, P, None)
                for s in range(2):
                    normalise(s, it * 2 + s, P)
                for s in range(2):
                    x_lo(s, it * 2 + s, P, ds((it * 2 + s) * P, P))
            scale_rows(0, NB, SMP, None)
            normalise(0, NB, SMP)
            x_lo(0, NB, SMP, slice(SEQ, NTOK))

            SB = 2 + SEQ

            def evac(i, d):
                k, c = d // 3, d % 3
                a, z = CH[c]
                src = bank(DN[d % 2], 0, z - a)
                v.wait_ge(dense_done, i * N_DENSE + d + 1)
                at = i * NTOK
                if k in (Q, K):
                    lo, hi = ((ql, qh), (kl, kh))[k]
                    v.wait_ge(evac_hi, i * 6 + d + 1)
                    V_.scalar_tensor_tensor(out=lo[:, a:z], in0=src, scalar=HD ** -0.5 if k == Q else 1.0, in1=f32(hi[:, a:z]),
                                            op0=ALU.mult, op1=ALU.subtract).then_inc(dense_free, 1)
                    if c == 2:
                        v.wait_ge(dense_free, i * N_DENSE + d + 1 + 2)
                        if k == Q:
                            for h in range(2):
                                r = slice(h * HD, h * HD + HD)
                                dst = qblk[r, :].rearrange("p (b x) -> p b x", x=QB)[:, :, h * NEW:h * NEW + NEW]
                                V_.tensor_tensor(dst, f32(qh[r, SEQ:NTOK]).rearrange("p (b t) -> p b t", t=NEW),
                                                 f32(ql[r, SEQ:NTOK]).rearrange("p (b t) -> p b t", t=NEW), ALU.add).then_inc(qblk_made, 1)
                        else:
                            V_.tensor_tensor(knew[:, :], f32(kh[:, SEQ:NTOK]), f32(kl[:, SEQ:NTOK]), ALU.add).then_inc(knew_made, 1)
                elif k == V:
                    if c == 0:
                        v.wait_ge(cu_out, i * (16 * (1 + NSEQ)) + 1)
                    V_.tensor_copy(vcu[:, a:z], src).then_inc(dense_free, 1)
                elif k == C:
                    V_.tensor_copy(br[:, ds(at + a, z - a)], src).then_inc(dense_free, 1)
                elif k == U:
                    if c == 0:
                        v.wait_ge(turn_full, i * N_TURN + turn_no[("v_out", 2)] + 1)
                        V_.memset(vcu[:, 0:2], 0.0).then_inc(pad_made, 1)
                    e = min(z, SEQ)
                    v.wait_ge(dense_free, i * N_DENSE + 3 * C + 3 + 2)
                    ins = V_.tensor_tensor(vcu[:, 2 + a:2 + e], ps[:, DN[d % 2] * 512:DN[d % 2] * 512 + e - a], br[:, ds(at + a, e - a)], ALU.mult)
                    if c == 2:
                        ins.then_inc(conv_step, 1)
                        x = DN[d % 2] * 512 + e - a
                        ins = V_.tensor_tensor(vcu[:, SB:NV].rearrange("p (b x) -> p b x", x=2 + NEW)[:, :, 2:2 + NEW],
                                               ps[:, x:x + SMP].rearrange("p (b t) -> p b t", t=NEW),
                                               br[:, ds(at + SEQ, SMP)].rearrange("p (b t) -> p b t", t=NEW), ALU.mult)
                    ins.then_inc(dense_free, 1)
                    if c == 2:
                        v.wait_ge(dense_free, i * N_DENSE + d + 1 + 2)
                        v.wait_ge(state_in, i * (16 * NSEQ) + 16 * NSEQ)
                        v.wait_ge(pad_made, i + 1)
                        v.wait_ge(conv_step, i * CONV_STEPS + 1)
                        wc = [cw[:, ds(i * 3 + w, 1)] for w in range(3)]
                        outs = (br[:, ds(at, SEQ)], br[:, ds(at + SEQ, SMP)].rearrange("p (b t) -> p b t", t=NEW))
                        ins_ = [(vcu[:, w:w + SEQ], vcu[:, SB:NV].rearrange("p (b x) -> p b x", x=2 + NEW)[:, :, w:w + NEW]) for w in range(3)]
                        for w in range(3):
                            for q in range(2):
                                if w == 0:
                                    op = V_.tensor_scalar(outs[q], ins_[w][q], wc[w], None, ALU.mult)
                                else:
                                    v.wait_ge(conv_step, i * CONV_STEPS + 1 + 2 * (w - 1) + q + 1)
                                    op = V_.scalar_tensor_tensor(out=outs[q], in0=ins_[w][q], scalar=wc[w], in1=outs[q], op0=ALU.mult, op1=ALU.add)
                                op.then_inc(conv_step, 1)
                elif k == B:
                    if c == 0:
                        v.wait_ge(conv_step, i * CONV_STEPS + CONV_STEPS)
                    V_.tensor_tensor(br[:, ds(at + a, z - a)], src, br[:, ds(at + a, z - a)], ALU.mult).then_inc(dense_free, 1)

            def p1(i):
                def turned(e):
                    v.wait_ge(turn_full, i * N_TURN + turn_no[e] + 1)

                for e in order:
                    if e[0] == "dense":
                        if 3 * e[1] + e[2] > 0:
                            evac(i, 3 * e[1] + e[2] - 1)
                    elif e[0] == "new_z":
                        turned(e)
                        V_.scalar_tensor_tensor(out=zc[0][:, PAST:KEYS], in0=bank(TURN, 0, SMP), scalar=bias_s[:, ds(i, 1)],
                                                in1=new_cap[:, :], op0=ALU.add, op1=ALU.min).then_inc(new_z_read, 1)
                    elif e[0] == "logits":
                        u = e[1]
                        W = width(u)
                        if u == 0:
                            v.wait_ge(turned_used, i * N_RING + 2 * NSEQ + 2)
                            v.wait_ge(new_z_read, i + 1)
                            V_.tensor_scalar(zc[0][:, 0:PAST], ps[:, ZS * 512:ZS * 512 + PAST], bias_s[:, ds(i, 1)], Z_MAX,
                                             ALU.add, ALU.min).then_inc(zc_ready, 1)
                        else:
                            h = (u - 1) // NB
                            v.wait_ge(z_full, i * (2 * NB) + u)
                            bias = bias_p[:, ds(i * 2 + h, 1)]
                            if W > P:
                                V_.tensor_scalar(zc[u % 3][:, 0:W - P], ps[:, ZP * 512:ZP * 512 + W - P], bias, Z_MAX, ALU.add, ALU.min)
                            V_.scalar_tensor_tensor(out=zc[u % 3][:, W - P:W], in0=ps[:, ZP * 512 + W - P:ZP * 512 + W], scalar=bias,
                                                    in1=diag_cap[:, :], op0=ALU.add, op1=ALU.min).then_inc(zc_ready, 1)
                    elif e[0] == "weights":
                        u = e[1]
                        W = width(u)
                        rev = sp[u % 2][:, 0:W][:, ::-1]
                        v.wait_ge(sp_made, i * UNITS + u + 1)
                        V_.tensor_tensor_scan(rev, rev, rev, 0.0, ALU.add, ALU.bypass).then_inc(suffix_made, 1)
                        v.wait_ge(suffix_made, i * UNITS + u + 1)
                        V_.tensor_tensor(zc[u % 3][:, 0:W], zc[u % 3][:, 0:W], sp[u % 2][:, 0:W], ALU.subtract).then_inc(arg_made, 1)
                    elif e[0] == "turn" and e[1] > 0:
                        u, (a, z) = e[1], groups(e[1])[e[2]]
                        s, w = ring_no[e] % 2, (z - a) * P
                        v.wait_ge(th_made, i * N_W + w_no[e] + 1)
                        V_.tensor_tensor(tl[s][:, 0:w], bank(TURN, 0, w), f32(th[s][:, 0:w]), ALU.subtract).then_inc(tl_made, 1)
                    elif e[0] == "v_out":
                        m = 3 + e[1]
                        s = m % 2
                        v.wait_ge(stage_made, i * 6 + m + 1)
                        if e[1] < 2:
                            src = stage[s][:, :].rearrange("p (b h d) -> p b h d", h=2, d=HD)
                            dst = vhl[:, e[1] * GRAN * 2 * P:(e[1] + 1) * GRAN * 2 * P].rearrange("p (b h x d) -> p b h x d", h=2, x=2, d=HD)
                            for h in range(2):
                                V_.tensor_copy(dst[:, :, h, h, :], src[:, :, h, :]).then_inc(vh_made, 1)
                            v.wait_ge(vh_made, i * 4 + 2 * e[1] + 2)
                            V_.tensor_tensor(dst[:, :, 0, 1, :], src[:, :, 0, :], f32(dst[:, :, 0, 0, :]), ALU.subtract)
                            V_.tensor_tensor(dst[:, :, 1, 0, :], src[:, :, 1, :], f32(dst[:, :, 1, 1, :]), ALU.subtract).then_inc(v_made, 1)
                        else:
                            V_.tensor_copy(vnew[:, :], stage[s][0:SMP, 0:P]).then_inc(v_made, 1)
                    elif e[0] == "av":
                        u, (a, z) = e[1], groups(e[1])[e[2]]
                        h, t = (u - 1) // NB, (u - 1) % NB
                        if z == t + 1 and t % 2 == 1:
                            r = slice(h * HD, h * HD + HD)
                            v.wait_ge(otmp_made, i * NB + h * (NB // 2) + t // 2 + 1)
                            V_.tensor_tensor(br[r, ds(i * NTOK + (4 * NTOK + (t - 1) * P), 2 * P)], ps[r, AVB * 512:AVB * 512 + 2 * P],
                                             otmp[r, :], ALU.add).then_inc(o_made, 1)
                    elif e[0] == "sample_o":
                        turned(e)
                        for h in range(2):
                            r = slice(h * HD, h * HD + HD)
                            ins = V_.tensor_copy(br[r, ds(i * NTOK + (4 * NTOK + SEQ), SMP)].rearrange("p (b t) -> p b t", t=NEW),
                                                 bank(TURN, 0, P)[r, :].rearrange("p (b x) -> p b x", x=2 * NEW)[:, :, h * NEW:h * NEW + NEW])
                        ins.then_inc(so_made, 1)
                evac(i, N_DENSE - 1)

            with v.Fori(0, NPAIR) as i:
                p1(i)

            for k in range(KT):
                x = slice(k * NTOK, (k + 1) * NTOK)
                v.wait_ge(b_hi, k + 1)
                V_.tensor_tensor(bl[:, x], br[:, x], f32(bh[:, x]), ALU.subtract).then_inc(b_lo, 1)
            v.wait_ge(b_lo, KT)
            with v.Fori(0, KT // 2) as j:
                for h in range(2):
                    for c in range(3):
                        d, (a, z) = 3 * h + c, CH[c]
                        w = z - a
                        m = mg[:, ds(j * (2 * NTOK) + (h * NTOK + a), w)]
                        v.wait_ge(proj_done, j * 6 + d + 1)
                        v.wait_ge(gate_free, j * 12 + 6 * h + c + 3 + 1 + 2)
                        V_.tensor_tensor(m, bank(2 + 2 * (d % 2), 0, w), sgc[:, a:z], ALU.mult).then_inc(gated_c, 1)
                        V_.tensor_tensor(sga[:, a:z], bank(3 + 2 * (d % 2), 0, w), sga[:, a:z], ALU.mult).then_inc(gated_a, 1)
                        v.wait_ge(gated_c, j * 6 + d + 1)
                        v.wait_ge(gated_a, j * 6 + d + 1)
                        V_.tensor_tensor(m, m, sga[:, a:z], ALU.add).then_inc(m_made, 1)
            for c in range(3):
                a, z = CH[c]
                v.wait_ge(m_hi, c + 1)
                V_.tensor_tensor(blocks(ml, NTOK)[:, :, a:z], blocks(mg, NTOK)[:, :, a:z], f32(blocks(mh, NTOK)[:, :, a:z]),
                                 ALU.subtract).then_inc(m_lo, 1)

            V_.memset(ssq[:, :], 0.0).then_inc(ssq_made, 1)
            with v.Fori(0, KT // 2) as j:
                for h in range(2):
                    f = j * 2 + h
                    for c in range(3):
                        n, (a, z) = 3 * h + c, CH[c]
                        x = x1[:, ds(f * NTOK + a, z - a)]
                        y = ds(f * NTOK + a, z - a)
                        v.wait_ge(xt_free, j * 6 + 3 * h + 3 + 2)
                        v.wait_ge(step_done, j * 6 + n + 1)
                        V_.tensor_tensor(x, bank(n, 0, z - a), x, ALU.add).then_inc(step_free, 1)
                        v.wait_ge(step_free, j * 6 + n + 1 + 6)
                        v.wait_ge(y_hi, j * 6 + n + 1)
                        V_.scalar_tensor_tensor(out=yl[:, y], in0=x, scalar=w2c[:, ds(f, 1)], in1=f32(yh[:, y]),
                                                op0=ALU.mult, op1=ALU.subtract).then_inc(y_lo, 1)
                        v.wait_ge(sq_made, j * 6 + n + 1)
                        v.wait_ge(ssq_made, j * 6 + n + 1)
                        V_.tensor_tensor(ssq[:, a:z], ssq[:, a:z], sqt[:, 0:z - a], ALU.add).then_inc(ssq_made, 1)
            for c in range(3):
                a, z = CH[c]
                v.wait_ge(rms_root, c + 1)
                V_.reciprocal(rms[:, a:z], rms[:, a:z]).then_inc(rms_made, 1)
            v.wait_ge(rms_made, 3)

            with v.Fori(0, NQ) as g:
                with v.Fori(0, KT // 2) as j:
                    def low(n):
                        a, z = CH[n % 3]
                        y = ds((j * 2 + n // 3) * NTOK + a, z - a)
                        v.wait_ge(h_hi, g * (3 * KT) + j * 6 + n + 1)
                        V_.tensor_tensor(hl[:, y], ts_[n % 2][:, 0:z - a], f32(hh[:, y]), ALU.subtract).then_inc(h_lo, 1)

                    for n in range(6):
                        a, z = CH[n % 3]
                        v.wait_ge(step_done, g * (6 * KT) + j * 6 + 3 * KT + n + 1)
                        V_.scalar_tensor_tensor(out=tt[n % 2][:, 0:z - a], in0=bank(n, 0, z - a), scalar=0.0, in1=rms[:, a:z],
                                                op0=ALU.max, op1=ALU.mult).then_inc(step_free, 1)
                        if n >= 1:
                            low(n - 1)
                    low(5)
                with v.Fori(0, KT // 2) as j:
                    for n in range(6):
                        a, z = CH[n % 3]
                        x = x1[:, ds((j * 2 + n // 3) * NTOK + a, z - a)]
                        v.wait_ge(step_done, g * (6 * KT) + j * 6 + 6 * KT + n + 1)
                        V_.tensor_tensor(x, bank(n, 0, z - a), x, ALU.add).then_inc(step_free, 1)

            v.wait_ge(wf_in, 16)
            for b in range(NB + 1):
                n, r, s = (P if b < NB else SMP), stat[b % 2], b % NY
                v.wait_ge(f_squared, b + 1)
                V_.tensor_scalar(r[0:n, 1:2], r[0:n, 0:1], 1.0 / D, EPS, ALU.mult, ALU.add).then_inc(f_mean, 1)
                v.wait_ge(f_root, b + 1)
                V_.reciprocal(r[0:n, 3:4], r[0:n, 2:3]).then_inc(f_rec, 1)
                v.wait_ge(f_rec, b + 1)
                if b >= NY:
                    v.wait_ge(y_out[s], 16 * (b // NY))
                V_.scalar_tensor_tensor(out=yst[s][0:n, :], in0=ps[0:n, (b % 4) * 1024:(b % 4) * 1024 + D], scalar=r[0:n, 3:4],
                                        in1=wfb[0:n, :], op0=ALU.mult, op1=ALU.mult).then_inc(y_made, 1)


INPUTS = ["x_prompt", "x_sample", "cache_k", "cache_v", "state_conv", "page_table", "norm1_w", "w_in", "conv_w",
          "w_proj_conv", "w_proj_attn", "att_bias", "w_out", "norm2_w", "w_up", "w_down", "norm_f_w"]


def kernel(**inputs):
    import numpy as np
    import concourse.bacc as bacc
    from concourse.bass_utils import run_bass_kernel_spmd as run

    xp, xs, page = inputs["x_prompt"].shape, inputs["x_sample"].shape, inputs["cache_k"].shape
    dc = inputs["state_conv"].shape[3]
    paged = (1, xp[0], xp[1] // page[2], page[2], page[3], page[4])
    new = (1, xs[0], xs[1], page[3], page[4])
    shapes = [("y_prompt", xp), ("y_sample", xs), ("k_prompt", paged), ("v_prompt", paged), ("conv_prompt", (1, xp[0], 2, dc)),
              ("k_sample", new), ("v_sample", new), ("conv_sample", (1, xs[0], 2, dc))]
    nc = bacc.Bacc("TRN2", target_bir_lowering=False, num_devices=1)
    arrays, args = {}, []
    for name in INPUTS:
        a = np.ascontiguousarray(inputs[name])
        arrays["in_" + name] = a
        args.append(nc.dram_tensor("in_" + name, a.shape, mybir.dt.from_np(a.dtype), kind="ExternalInput").ap())
    for name, shape in shapes:
        args.append(nc.dram_tensor("out_" + name, shape, F32, kind="ExternalOutput").ap())
    hybrid_layer(nc, *args)
    r = run(nc, [arrays], core_ids=[0])
    return tuple(r.results[0]["out_" + name] for name, _ in shapes)
```

```python
from contextlib import ExitStack

import concourse.bass as bass
from concourse import mybir

F32 = mybir.dt.float32
F32R = mybir.dt.float32r
I32 = mybir.dt.int32
ALU = mybir.AluOpType
ACT = mybir.ActivationFunctionType

P = 128
EPS = 1e-6
Z_MAX = 40.0
MASKED = -1e30
Q, K, V, C, U, B = range(6)
GRAN = 4
N_CONST = 6
N_EARLY, N_STEPS = 5, 79
CONV_STEPS = 7


def ds(start, size):
    return bass.ds(start, size)


def hybrid_layer(nc, x_prompt, x_sample, cache_k, cache_v, state_conv, page_table, norm1_w, w_in, conv_w,
                 w_proj_conv, w_proj_attn, att_bias, w_out, norm2_w, w_up, w_down, norm_f_w,
                 y_prompt, y_sample, k_prompt, v_prompt, conv_prompt, k_sample, v_sample, conv_sample):
    _, SEQ, D = x_prompt.shape
    NSEQ, NEW, _ = x_sample.shape
    _, N_POOL, PAGE, NH, HD = cache_k.shape
    N_PAGES = page_table.shape[1]
    DC = state_conv.shape[3]
    D_FF = w_up.shape[2]
    SMP = NSEQ * NEW
    NTOK = SEQ + SMP
    KT = D // P
    NB = SEQ // P
    NPAIR = NH * HD // P
    PAST = N_PAGES * PAGE
    KEYS = PAST + SMP
    NQ = D_FF // D
    NITER = NSEQ // 2
    assert PAGE == P and 2 * HD == P and DC == NPAIR * P and NB == 8 and PAST == 8 * P and 2 * NEW * NSEQ == P
    CH = [(0, 364), (364, 728), (728, NTOK)]
    COL = {Q: 3 * DC, K: 3 * DC + D // 2, V: 3 * DC + D, C: DC, U: 2 * DC, B: 0}
    COL_GC, COL_GA = 3 * DC + 3 * NH * HD, 3 * DC + 3 * NH * HD + D

    xp = x_prompt.rearrange("o (a p) n -> p (o a) n", p=P)
    xs = x_sample.rearrange("b t n -> (b t) n")
    yp = y_prompt.rearrange("o (a p) n -> p (o a) n", p=P)
    ys = y_sample.rearrange("b t n -> (b t) n")
    ck = cache_k.rearrange("o n p h d -> (o n) p (h d)")
    cv = cache_v.rearrange("o n p h d -> (o n) p (h d)")
    kv_out = {K: (k_prompt.rearrange("o b a p h d -> p (o b a) (h d)"), k_sample.rearrange("o b t h d -> (o b t) (h d)")),
              V: (v_prompt.rearrange("o b a p h d -> p (o b a) (h d)"), v_sample.rearrange("o b t h d -> (o b t) (h d)"))}
    st = state_conv.rearrange("o b w c -> c (o b) w")
    cp = conv_prompt.rearrange("o b w c -> c (o b w)")
    cs = conv_sample.rearrange("o b w c -> c (o b) w")

    def rows(w):
        return w.rearrange("o (k p) n -> p (o k) n", p=P)

    win, wpc, wpa, wo, wup, wdn = map(rows, (w_in, w_proj_conv, w_proj_attn, w_out, w_up, w_down))

    ctx = ExitStack()
    with ctx:
        cursor = [(nc.sbuf_base + 31) // 32 * 32]

        def place(name, shape, dt, at=None):
            size = 4
            for n in shape[1:]:
                size *= n
            off = cursor[0] if at is None else at
            if at is None:
                cursor[0] += (size + 31) // 32 * 32
            return nc.alloc_sbuf_tensor_at(name, shape, dt, offset=off)

        ident = place("ident", [P, P], F32)
        identr = place("identr", [P, P], F32R)
        ones = place("ones", [P, P], F32)
        diag_cap = place("diag_cap", [P, P], F32)
        new_cap = place("new_cap", [P, NITER * SMP], F32)
        bias_p = place("bias_p", [P, NH], F32)
        bias_s = place("bias_s", [P, 1], F32)
        w2c = place("w2c", [P, KT], F32)
        cw = place("cw", [P, NPAIR * 3], F32)
        eps = place("eps", [P, 1], F32)
        pages = place("pages", [1, NSEQ * N_PAGES], I32)
        stats = place("stats", [P, 3 * (NB + 1)], F32)
        stat = [stats[:, 3 * b:3 * b + 3] for b in range(NB + 1)]

        raw = [place(f"raw{s}", [P, KT * P], F32) for s in range(2)]
        wh = [place(f"wh{s}", [P, KT * P], F32R) for s in range(2)]
        wl = [place(f"wl{s}", [P, KT * P], F32R) for s in range(2)]

        WIDE = KT * NTOK
        r1 = cursor[0]
        xh = place("xh", [P, WIDE], F32R)
        r1b = cursor[0]
        xl = place("xl", [P, WIDE], F32R)
        mh, ml = place("mh", [P, WIDE], F32R, r1), place("ml", [P, WIDE], F32R, r1b)
        hh, hl = place("hh", [P, WIDE], F32R, r1), place("hl", [P, WIDE], F32R, r1b)
        r3 = cursor[0]
        br = place("br", [P, WIDE], F32)
        mg = place("mg", [P, WIDE], F32, r3)
        x1 = place("x1", [P, WIDE], F32, r3)
        r2 = cursor[0]
        bh, bl = place("bh", [P, WIDE], F32R), place("bl", [P, WIDE], F32R)
        yh, yl = place("yh", [P, WIDE], F32R, r2), place("yl", [P, WIDE], F32R, r2 + 4 * WIDE)
        r4 = cursor[0]
        CW = 364
        sgc, sga = place("sgc", [P, NTOK], F32), place("sga", [P, NTOK], F32)
        ssq = place("ssq", [P, NTOK], F32, r4)
        sqt = place("sqt", [P, CW], F32, r4 + 4 * NTOK)
        CWB = -(-4 * CW // 32) * 32
        XIN = r4 + 4 * NTOK + CWB
        xin = place("xin", [P, (NB + 1) * P], F32, XIN)
        tt = [place(f"tt{s}", [P, CW], F32, r4 + s * CWB) for s in range(2)]
        ts_ = [place(f"ts{s}", [P, CW], F32, r4 + (2 + s) * CWB) for s in range(2)]
        rms = place("rms", [P, NTOK], F32, r4 + 4 * CWB)
        assert max(XIN + 4 * (NB + 1) * P, r4 + 4 * CWB + 4 * NTOK) <= nc.sbuf_usable_end
        NY = 3
        yst = [place(f"yst{s}", [P, D], F32, r1 + s * 4 * D) for s in range(NY)]
        sqf = place("sqf", [P, D], F32, r1 + NY * 4 * D)
        wfb = place("wfb", [P, D], F32, r2)
        cursor[0] = r2
        qs = place("qs", [P, NPAIR * SMP], F32)
        ks = place("ks", [P, NPAIR * SMP], F32)
        vs = place("vs", [SMP, NPAIR * P], F32)
        scratch = cursor[0]
        qh, ql = place("qh", [P, SEQ], F32R), place("ql", [P, SEQ], F32R)
        kh, kl = place("kh", [P, NTOK], F32R), place("kl", [P, NTOK], F32R)
        vhl = place("vhl", [P, NB * 2 * P], F32R)
        NV = 2 + SEQ + NSEQ * (2 + NEW)
        vcu = place("vcu", [P, NV], F32)
        NZ, NT = 4, 4
        zc = [place(f"zc{s}", [P, SEQ], F32) for s in range(NZ)]
        sp = [place(f"sp{s}", [P, SEQ], F32) for s in range(2)]
        th = [place(f"th{s}", [P, 512], F32R) for s in range(NT)]
        tl = [place(f"tl{s}", [P, 512], F32R) for s in range(NT)]
        stage = [place(f"stage{s}", [P, GRAN * P], F32) for s in range(2)]
        otmp = place("otmp", [P, 2 * P], F32)
        assert cursor[0] <= nc.sbuf_usable_end, cursor[0] - nc.sbuf_usable_end
        cursor[0] = scratch
        ROWS = NPAIR * 2 * NEW
        NWIN = 2 * NPAIR
        WIN = P + 2 * NEW
        qblk = place("qblk", [P, NWIN * WIN], F32)
        kct = [place(f"kct{s}", [P, NPAIR * 512], F32) for s in range(2)]
        zs_c = place("zs_c", [P, KEYS], F32)
        sp_s = place("sp_s", [P, KEYS], F32)
        swT = place("swT", [P, (N_PAGES + 1) * P], F32)
        so = [place(f"so{s}", [ROWS, NPAIR * P], F32) for s in range(2)]
        cache = [place(f"cache{s}", [P, GRAN * NPAIR * P], F32) for s in range(4)]
        assert cursor[0] <= nc.sbuf_usable_end, cursor[0] - nc.sbuf_usable_end
        cursor[0] = r2
        xr = place("xr", [P, (NB + 1) * D], F32)
        sq0 = place("sq0", [P, D], F32)
        w1b = place("w1b", [P, D], F32)

        def f32(t):
            return t.bitcast(F32)

        def blocks(t, n=P):
            return t.rearrange("p (k n) -> p k n", n=n)

        ps = ctx.enter_context(nc.psum_tensor("ps", [P, 8 * 512], F32))

        X_BANK = [2 + 2 * (b % 3) for b in range(NB + 1)]

        def bank(b, a=0, e=512):
            return ps[:, b * 512 + a:b * 512 + e]

        ZB, TURN, AVB = 3, 5, 7

        credits = []

        def sem(name, credit=0):
            s = ctx.enter_context(nc.semaphore(name))
            if credit:
                credits.append((s, credit))
            return s

        consts_in = sem("consts_in")
        const_step = sem("const_step")
        w1_in, bias_in = sem("w1_in"), sem("bias_in")
        identr_made = sem("identr_made")
        raw_in = [sem(f"raw_in{s}") for s in range(2)]
        w_hi = sem("w_hi")
        w_split = sem("w_split", 2)
        passed = sem("passed")
        x_in = [sem(f"x_in{s}") for s in range(NB // 2 + 1)]
        x_squared, x_root, x_rec, x_scaled, x_turned, xh_done, xl_done = (
            sem(n) for n in ("x_squared", "x_root", "x_rec", "x_scaled", "x_turned", "xh_done", "xl_done"))
        dense_done = sem("dense_done")
        dense_free = sem("dense_free", 3)
        evac_hi = sem("evac_hi")
        turn_full = sem("turn_full")
        turned_used = sem("turned_used", NT)
        th_made, tl_made = sem("th_made"), sem("tl_made", 2)
        z_full = sem("z_full")
        zc_ready = sem("zc_ready", 1)
        exp_done, sp_made, suffix_made, arg_made, w_made = (sem(n) for n in ("exp_done", "sp_made", "suffix_made", "arg_made", "w_made"))
        stage_made = sem("stage_made")
        stage_out = [sem(f"stage_out{s}", 1) for s in range(2)]
        vh_made, v_made = sem("vh_made"), sem("v_made")
        otmp_made, o_made = sem("otmp_made"), sem("o_made", 1)
        qs_made, ks_made = sem("qs_made"), sem("ks_made")
        state_in = sem("state_in")
        pad_made, conv_step = sem("pad_made"), sem("conv_step")
        cu_out = sem("cu_out", 1)
        page_in = [sem(f"page_in{s}") for s in range(4)]
        page_used = sem("page_used", 4)
        qblk_zero, qblk_made = sem("qblk_zero"), sem("qblk_made")
        s_turned = sem("s_turned")
        kct_made = sem("kct_made", 2)
        new_z_full = sem("new_z_full")
        new_z_read = sem("new_z_read", 1)
        s_zc = sem("s_zc", 1)
        s_exp, s_sp, s_suffix, s_arg, s_w = (sem(n) for n in ("s_exp", "s_sp", "s_suffix", "s_arg", "s_w"))
        swt_made = sem("swt_made")
        so_full, so_copied, so_made = sem("so_full"), sem("so_copied"), sem("so_made", 1)
        b_hi, b_lo = sem("b_hi"), sem("b_lo")
        gate_done, proj_done = sem("gate_done"), sem("proj_done")
        gate_free = sem("gate_free", 2)
        gated_c, gated_a = sem("gated_c"), sem("gated_a")
        m_made = sem("m_made", 3)
        m_hi, m_lo = sem("m_hi"), sem("m_lo")
        xin_in = sem("xin_in")
        xt_turned = sem("xt_turned")
        xt_free = sem("xt_free", 2)
        step_done = sem("step_done")
        step_free = sem("step_free", 6)
        y_hi, y_lo, sq_made, ssq_made = (sem(n) for n in ("y_hi", "y_lo", "sq_made", "ssq_made"))
        rms_sum, rms_root, rms_made = sem("rms_sum"), sem("rms_root"), sem("rms_made")
        s_made, h_hi, h_lo = (sem(n) for n in ("s_made", "h_hi", "h_lo"))
        wf_in = sem("wf_in")
        f_turned, f_squared, f_root, f_rec, y_made = (sem(n) for n in ("f_turned", "f_squared", "f_root", "f_rec", "y_made"))
        y_out = [sem(f"y_out{s}") for s in range(NY)]

        UNITS = 2 * NB

        UNIT = [(h, t) for top in range(NB - 1, 0, -2) for h in range(2) for t in (top, top - 1)]

        def width(u):
            return (UNIT[u][1] + 1) * P

        def groups(u):
            n = width(u) // P
            return [(a, min(a + GRAN, n)) for a in range(0, n, GRAN)]

        order = []
        dense = iter([(k, c) for k in range(6) for c in range(3)])

        def dense_step():
            order.append(("dense", *next(dense)))

        def unit_slot(n):
            def has(u):
                return 0 <= u < UNITS

            if has(n + 1):
                order.append(("logits", n + 1))
            if has(n):
                order.append(("softplus", n))
            if has(n - 1):
                order.append(("suffix", n - 1))
            if has(n - 3):
                order.extend(("low", n - 3, j) for j in range(len(groups(n - 3))))
            if has(n + 1):
                order.append(("cap", n + 1))
            if has(n - 1):
                order.append(("weights", n - 1))
            if has(n - 4):
                order.append(("out", n - 4))
            if taps:
                order.append(taps.pop(0))
            dense_half(n)
            if has(n - 2):
                order.extend(("turn", n - 2, j) for j in range(len(groups(n - 2))))
            if has(n - 3):
                order.extend(("av", n - 3, j) for j in range(len(groups(n - 3))))

        FIRST, LAST = 2, UNITS + 3
        N_LATE = 8
        late, taps = [], []

        def work(n):
            return 2 * P + sum(width(u) for u in (n + 1, n - 1, n - 2, n - 3) if 0 <= u < UNITS)

        total = sum(work(n) for n in range(FIRST, LAST + 1))

        def dense_half(n):
            seen = sum(work(m) for m in range(FIRST, n + 1))
            while n >= FIRST and len(late) < 2 * N_LATE and seen * 2 * N_LATE >= (len(late) + 1) * total * 0.84:
                half = len(late) % 2
                chunk = next(dense) if half == 0 else late[-1][1:]
                late.append((("first_half", "second_half")[half], *chunk))
                if late[-1] == ("first_half", B, 1):
                    order.extend(taps)
                    taps.clear()
                order.append(late[-1])
                if late[-1] == ("first_half", B, 0):
                    taps.extend(("conv", w) for w in range(3))

        for _ in range(7):
            dense_step()
        order.append(("k_out", 0))
        unit_slot(-1)
        dense_step()
        order += [("k_out", 1), ("k_out", 2)]
        unit_slot(0)
        dense_step()
        unit_slot(1)
        dense_step()
        order += [("v_out", j) for j in range(3)]
        for n in range(2, LAST + 1):
            unit_slot(n)
        assert next(dense, None) is None
        TURNS = [e for e in order if e[0] in ("k_out", "v_out", "turn")]
        turn_no = {e: n for n, e in enumerate(TURNS)}
        N_TURN = len(TURNS)
        W_TURNS = [e for e in order if e[0] == "turn"]
        w_no = {e: n for n, e in enumerate(W_TURNS)}
        N_W = len(W_TURNS)
        assert N_TURN % 2 == 0 and N_W % NT == 0 and UNITS % NZ == 0
        N_DENSE = 18
        P1_DENSE = NPAIR * N_DENSE
        S_TURNS = 4 * GRAN + 3 + 2

        K_TURNS = 4 * GRAN

        def key_use(j):
            return 0 if isinstance(j, int) and j == 0 else j * 2 - 1

        def value_use(j, last):
            return 2 * NITER - 1 if last else j * 2 + 2

        def newest_keys(j, last):
            return j if last else j + 1

        def out_use(j):
            return 0 if isinstance(j, int) and j == 0 else j - 1

        def turns_before(j):
            return 0 if isinstance(j, int) and j == 0 else S_TURNS - K_TURNS

        def s_weights_turned(j, last):
            return j * S_TURNS + (K_TURNS if last else 2 * K_TURNS)

        def apart(eng):
            eng.sem_inc(passed, 1)

        def p1a_done(eng):
            eng.wait_ge(o_made, NPAIR * NB + 1)
            eng.wait_ge(dense_free, P1_DENSE + 3)
            eng.wait_ge(turned_used, NPAIR * N_W + NT)
            for s in range(2):
                eng.wait_ge(stage_out[s], 48 * NPAIR + 1)
            eng.wait_ge(cu_out, 16 * (1 + NSEQ) * NPAIR + 1)

        block = ctx.enter_context(nc.Block())

        @block.sync
        def _(sp_):
            def weight_tile(t, slot, views, wait):
                sp_.wait_ge(w_split, wait)
                apart(sp_)
                dst = blocks(raw[slot])
                for half, view in enumerate(views):
                    sp_.dma_start(dst[:, half * 4:half * 4 + 4, :], view).then_inc(raw_in[slot], 16)

            def halves(w, k0, col):
                return [w[:, k0 + 4 * s:k0 + 4 * s + 4, ds(col, P)] for s in range(2)]

            sp_.dma_start(w1b[:, :], norm1_w.to_broadcast([P, D])).then_inc(w1_in, 16)
            for b in range(0, NB, 2):
                sp_.dma_start(blocks(xr, D)[:, b:b + 2, :], xp[:, b:b + 2, :]).then_inc(x_in[b // 2], 16)
            sp_.dma_start(xr[0:SMP, NB * D:(NB + 1) * D], xs).then_inc(x_in[NB // 2], 16)

            def store_rows(i, tile, j):
                s = (3 * (tile == V) + j) % 2
                sp_.wait_ge(stage_made, i * 6 + 3 * (tile == V) + j + 1)
                apart(sp_)
                prompt, sample = kv_out[tile]
                if j < 2:
                    sp_.dma_start(prompt[:, j * GRAN:(j + 1) * GRAN, ds(i * P, P)], blocks(stage[s])).then_inc(stage_out[s], 16)
                else:
                    sp_.dma_start(sample[:, ds(i * P, P)], stage[s][0:SMP, 0:P]).then_inc(stage_out[s], 16)

            with sp_.Fori(0, NPAIR) as i:
                for k in (Q, K):
                    weight_tile(None, k % 2, halves(win, 0, i * P + COL[k]), i * 6 + k + 1)
                for e in order:
                    if e[0] in ("dense", "first_half") and e[2] == 0 and e[1] < 4:
                        k = e[1] + 2
                        weight_tile(None, k % 2, halves(win, 0, i * P + COL[k]), i * 6 + k + 1)
                    if e[0] == "k_out":
                        store_rows(i, K, e[1])
                    if e[0] == "v_out":
                        store_rows(i, V, e[1])
                        if e[1] == 2:
                            sp_.wait_ge(turn_full, i * N_TURN + turn_no[("v_out", 2)] + 1)
                            apart(sp_)
                            with nc.allow_non_contiguous_dma(reason="two columns per sequence"):
                                for b in range(NSEQ):
                                    a = 2 + SEQ + b * (2 + NEW)
                                    sp_.dma_start(vcu[:, a:a + 2].rearrange("p (o w) -> p o w", o=1),
                                                  st[ds(i * P, P), b:b + 1, :]).then_inc(state_in, 16)
                sp_.wait_ge(dense_free, i * N_DENSE + 3 * U + 3 + 3)
                apart(sp_)
                with nc.allow_non_contiguous_dma(reason="two rows per sequence"):
                    sp_.dma_start(cp[ds(i * P, P), :], vcu[:, SEQ:SEQ + 2]).then_inc(cu_out, 16)
                    for b in range(NSEQ):
                        a = 2 + SEQ + b * (2 + NEW) + NEW
                        sp_.dma_start(cs[ds(i * P, P), b:b + 1, :],
                                      vcu[:, a:a + 2].rearrange("p (o w) -> p o w", o=1)).then_inc(cu_out, 16)

            with nc.allow_non_contiguous_dma(reason="small constants"):
                for n in range(P // NEW):
                    sp_.dma_start(bias_s[n * NEW:(n + 1) * NEW, :],
                                  att_bias[:, n % NH:n % NH + 1].to_broadcast([NEW, 1])).then_inc(bias_in, 16)
            sp_.wait_ge(consts_in, 16 * N_CONST)
            p1a_done(sp_)

            def page_groups(j, src, use):
                for g in range(4):
                    sp_.wait_ge(page_used, use * 4 + g + 1)
                    apart(sp_)
                    numbers = [sp_.value_load(pages[0:1, ds(j * (2 * N_PAGES) + g * GRAN + n, 1)]) for n in range(GRAN)]
                    for n, page in enumerate(numbers):
                        sp_.dma_start(cache[g][:, n * NPAIR * P:(n + 1) * NPAIR * P].rearrange("p (o n) -> p o n", o=1),
                                      src[ds(page, 1), :, :].rearrange("o p n -> p o n")).then_inc(page_in[g], 16)

            page_groups(0, ck, 0)
            with sp_.Fori(0, NITER - 1) as j:
                page_groups(j + 1, ck, j * 2 + 1)
                page_groups(j, cv, j * 2 + 2)
            page_groups(NITER - 1, cv, 2 * NITER - 1)

            base = 6 * NPAIR
            with sp_.Fori(0, KT // 2) as j:
                for h in range(2):
                    f = j * 2 + h
                    for k, views in enumerate((halves(win, 0, f * P + COL_GC), halves(win, 0, f * P + COL_GA),
                                               [wpc[:, 0:4, ds(f * P, P)], wpa[:, 0:4, ds(f * P, P)]])):
                        weight_tile(None, (3 * h + k) % 2, views, j * 6 + base + 3 * h + k + 1)
            base += 3 * KT
            with sp_.Fori(0, KT // 2) as j:
                for h in range(2):
                    f = j * 2 + h
                    weight_tile(None, h, halves(wo, 0, f * P), j * 2 + base + h + 1)
                    if h == 0:
                        sp_.wait_ge(m_made, 3 * KT + 3)
                    sp_.wait_ge(xt_free, j * 6 + 3 * h + 2)
                    apart(sp_)
                    sp_.dma_start(blocks(xin)[:, 0:NB, :], xp[:, :, ds(f * P, P)]).then_inc(xin_in, 16)
                    sp_.dma_start(xin[0:SMP, NB * P:], xs[:, ds(f * P, P)]).then_inc(xin_in, 16)
            base += KT
            with sp_.Fori(0, NQ) as g:
                with sp_.Fori(0, KT // 2) as j:
                    for h in range(2):
                        weight_tile(None, h, halves(wup, 0, g * D + j * (2 * P) + h * P), g * (2 * KT) + j * 2 + base + h + 1)
                with sp_.Fori(0, KT // 2) as j:
                    for h in range(2):
                        col = j * (2 * P) + h * P
                        weight_tile(None, h, [wdn[:, ds(g * KT + 4 * s, 4), ds(col, P)] for s in range(2)],
                                    g * (2 * KT) + j * 2 + base + KT + h + 1)
            sp_.wait_ge(step_done, 3 * (KT + 2 * KT * NQ))
            sp_.dma_start(wfb[:, :], norm_f_w.rearrange("(o n) -> o n", o=1).to_broadcast([P, D])).then_inc(wf_in, 16)
            for b in range(NB + 1):
                s = b % NY
                n = P if b < NB else SMP
                sp_.wait_ge(y_made, b + 1)
                sp_.dma_start(yp[:, b, :] if b < NB else ys, yst[s][0:n, :]).then_inc(y_out[s], 16)
            for s in range(NY):
                sp_.wait_ge(y_out[s], 16 * len(range(s, NB + 1, NY)))
            for s in range(2):
                sp_.wait_ge(stage_out[s], 16 * 3 * NPAIR + 1)
            sp_.wait_ge(cu_out, 16 * (1 + NSEQ) * NPAIR + 1)

        @block.gpsimd
        def _(pool):
            g = nc.gpsimd
            for s, n in credits:
                pool.sem_inc(s, n)
            steps = [0]

            def step(ins):
                steps[0] += 1
                ins.then_inc(const_step, 1)
                pool.wait_ge(const_step, steps[0])

            step(g.memset(ident[:, :], 1.0))
            step(g.affine_select(out=ident[:, :], in_=ident[:, :], compare_op=ALU.is_equal, fill=0.0, base=0,
                                 pattern=[[-1, P]], channel_multiplier=1))
            step(g.memset(diag_cap[:, :], Z_MAX))
            step(g.affine_select(out=diag_cap[:, :], in_=diag_cap[:, :], compare_op=ALU.is_gt, fill=MASKED, base=0,
                                 pattern=[[-1, P]], channel_multiplier=1))
            step(g.memset(eps[:, :], EPS))
            assert steps[0] == N_EARLY

            def split(t2, s, used):
                pool.wait_ge(raw_in[s], t2 * 32 + 32)
                if used is not None:
                    pool.wait_ge(*used)
                apart(pool)
                g.tensor_copy(wh[s][:, :], raw[s][:, :]).then_inc(w_hi, 1)
                return s

            def split_lo(s, t):
                pool.wait_ge(w_hi, t + 1)
                apart(pool)
                g.tensor_tensor(wl[s][:, :], raw[s][:, :], f32(wh[s][:, :]), ALU.subtract).then_inc(w_split, 1)

            for t in range(2):
                split(0, t, None)
                split_lo(t, t)
            for n in range(P // NEW):
                cap = ones[:, 0:NEW] if n == 0 else ones[:, NEW:2 * NEW]
                step(g.memset(cap, 0.0))
                step(g.affine_select(out=cap, in_=cap, compare_op=ALU.is_gt, fill=1.0, base=-NEW * n,
                                     pattern=[[-1, NEW]], channel_multiplier=1))
                step(g.affine_select(out=cap, in_=cap, compare_op=ALU.is_ge, fill=1.0, base=NEW - 1 + NEW * n,
                                     pattern=[[0, NEW]], channel_multiplier=-1))
                if n:
                    step(g.tensor_tensor(ones[:, 0:NEW], ones[:, 0:NEW], cap, ALU.mult))
            step(g.tensor_scalar(ones[:, 0:NEW], ones[:, 0:NEW], MASKED, Z_MAX, ALU.mult, ALU.add))
            step(g.memset(new_cap[:, :], MASKED))
            for j in range(NITER):
                for n in range(2):
                    at = j * SMP + (2 * j + n) * NEW
                    step(g.tensor_copy(new_cap[n * ROWS:(n + 1) * ROWS, at:at + NEW], ones[n * ROWS:(n + 1) * ROWS, 0:NEW]))
            step(g.memset(ones[:, :], 1.0))
            with g.Fori(1, 3 * NPAIR) as j:
                for s in range(2):
                    split(j, s, (dense_done, j * 6 + 3 * s - 6 + 3))
                    split_lo(s, j * 2 + s)
            T0 = 3 * NPAIR
            for t in range(2):
                split(T0, t, (dense_done, P1_DENSE - 3 + 3 * t))
                split_lo(t, 2 * T0 + t)

            def p2_tile(j, n, used):
                split(j * 3 + (T0 + n // 2), n % 2, used)
                split_lo(n % 2, j * 6 + (2 * T0 + n))

            def p2_rest(j):
                p2_tile(j, 2, (gate_done, j * 12 + 3))
                p2_tile(j, 3, (gate_done, j * 12 + 6))
                p2_tile(j, 4, (proj_done, j * 6 + 3))
                p2_tile(j, 5, (gate_done, j * 12 + 9))
            p2_rest(0)
            with g.Fori(1, KT // 2) as j:
                p2_tile(j, 0, (gate_done, j * 12))
                p2_tile(j, 1, (proj_done, j * 6))
                p2_rest(j)
            T1 = T0 + 3 * KT // 2
            split(T1, 0, (gate_done, 6 * KT))
            split_lo(0, 2 * T1)
            split(T1, 1, (proj_done, 3 * KT))
            split_lo(1, 2 * T1 + 1)
            with g.Fori(1, (KT + 2 * KT * NQ) // 2) as j:
                for s in range(2):
                    split(j + T1, s, (step_done, j * 6 + 3 * s - 6 + 3))
                    split_lo(s, j * 2 + (2 * T1 + s))

        @block.tensor
        def _(pe):
            mm, tr = nc.tensor.matmul, nc.tensor.transpose

            def product(out, w, lo_w, ks, mov_h, mov_l, cols, first=True, last=True):
                n = len(ks)
                for a, k in enumerate(ks):
                    x = slice(k * NTOK + cols[0], k * NTOK + cols[1])
                    for m, (lhs, rhs) in enumerate(((w, mov_h), (w, mov_l), (lo_w, mov_h))):
                        ins = mm(out, lhs[:, k * P:(k + 1) * P], rhs[:, x], start=(first and a == 0 and m == 0),
                                 stop=(last and a == n - 1 and m == 2))
                return ins

            def width_of(c):
                return CH[c][1] - CH[c][0]

            for b in range(NB + 1):
                n, at = (P if b < NB else SMP), X_BANK[b] * 512
                if b == 0:
                    pe.wait_ge(const_step, N_EARLY)
                pe.wait_ge(x_scaled, b + 1)
                if b >= 3:
                    pe.wait_ge(xl_done, b - 2)
                for f in range(KT):
                    ins = tr(ps[:, at + f * P:at + f * P + n], xr[0:n, b * D + f * P:b * D + (f + 1) * P], ident[0:n, 0:n])
                ins.then_inc(x_turned, 1)
            pe.wait_ge(identr_made, 1)

            def p1a(i):
                def turn_bank(e):
                    n = turn_no[e]
                    last = TURNS[n - 2]
                    if n < 2 or last[0] == "turn":
                        pe.wait_ge(tl_made, i * N_W + (n if n < 2 else w_no[last] + 1 + 1) + 1)
                    else:
                        pe.wait_ge(stage_made, i * 6 + 3 * (last[0] == "v_out") + last[1] + 1)
                    return TURN + n % 2

                for e in order:
                    if e[0] == "dense":
                        _, k, c = e
                        d = 3 * k + c
                        pe.wait_ge(w_split, i * 6 + k + 1 + 2)
                        pe.wait_ge(dense_free, i * N_DENSE + d + 1)
                        if k == Q:
                            pe.wait_ge(xl_done, -(-CH[c][1] // P))
                        product(bank(c, 0, width_of(c)), wh[k % 2], wl[k % 2], range(KT), xh, xl, CH[c]).then_inc(dense_done, 1)
                    elif e[0] == "first_half":
                        _, k, c = e
                        pe.wait_ge(w_split, i * 6 + k + 1 + 2)
                        pe.wait_ge(dense_free, i * N_DENSE + 3 * k + c + 1)
                        product(bank(c, 0, width_of(c)), wh[k % 2], wl[k % 2], range(KT // 2), xh, xl, CH[c], last=False)
                    elif e[0] == "second_half":
                        _, k, c = e
                        product(bank(c, 0, width_of(c)), wh[k % 2], wl[k % 2], range(KT // 2, KT), xh, xl, CH[c],
                                first=False).then_inc(dense_done, 1)
                    elif e[0] == "k_out":
                        tb = turn_bank(e) * 512
                        pe.wait_ge(dense_free, i * N_DENSE + 3 * K + 3 + 3)
                        for b in range(GRAN * e[1], min(GRAN * e[1] + GRAN, NB + 1)):
                            n = P if b < NB else SMP
                            out = ps[0:n, tb + (b % GRAN) * P:tb + (b % GRAN) * P + P]
                            mm(out, kh[:, b * P:b * P + n], identr[:, :], start=True, stop=False)
                            ins = mm(out, kl[:, b * P:b * P + n], identr[:, :], start=False, stop=True)
                        ins.then_inc(turn_full, 1)
                    elif e[0] == "v_out":
                        tb = turn_bank(e) * 512
                        pe.wait_ge(dense_free, i * N_DENSE + 3 * V + 3 + 3)
                        apart(pe)
                        for b in range(GRAN * e[1], min(GRAN * e[1] + GRAN, NB + 1)):
                            n = P if b < NB else SMP
                            ins = tr(ps[0:n, tb + (b % GRAN) * P:tb + (b % GRAN) * P + P], vcu[:, b * P:b * P + n], ident[:, :])
                        ins.then_inc(turn_full, 1)
                    elif e[0] == "logits":
                        u = e[1]
                        h, t = UNIT[u]
                        r = slice(h * HD, h * HD + HD)
                        pe.wait_ge(zc_ready, i * UNITS + u + 1)
                        if u == 0:
                            pe.wait_ge(dense_free, i * N_DENSE + 3 * K + 3 + 3)
                        for a in range(0, width(u), 512):
                            z = min(width(u), a + 512)
                            for m, (x, y) in enumerate(((qh, kh), (qh, kl), (ql, kh))):
                                ins = mm(ps[:, ZB * 512 + a:ZB * 512 + z], x[r, t * P:(t + 1) * P], y[r, a:z],
                                         start=(m == 0), stop=(m == 2))
                        ins.then_inc(z_full, 1)
                    elif e[0] == "turn":
                        u, (a, z) = e[1], groups(e[1])[e[2]]
                        tb = turn_bank(e)
                        if e[2] == 0:
                            pe.wait_ge(w_made, i * UNITS + u + 1)
                        for j in range(a, z):
                            ins = tr(bank(tb, (j - a) * P, (j - a + 1) * P), zc[u % NZ][:, j * P:(j + 1) * P], ident[:, :])
                        ins.then_inc(turn_full, 1)
                    elif e[0] == "av":
                        u, (a, z) = e[1], groups(e[1])[e[2]]
                        h, t = UNIT[u]
                        key = ("turn", u, e[2])
                        s = w_no[key] % NT
                        if e[2] == 0 and u % 2 == 0:
                            pe.wait_ge(o_made, i * NB + u // 2 + 1)
                        pe.wait_ge(tl_made, i * N_W + w_no[key] + 1 + 2)
                        if u == 0:
                            pe.wait_ge(v_made, i * 3 + 3)
                        out = bank(AVB, (t % 2) * P, (t % 2) * P + P)
                        for j in range(a, z):
                            v = vhl[:, (j * 2 + h) * P:(j * 2 + h + 1) * P]
                            mm(out, v, th[s][:, (j - a) * P:(j - a + 1) * P], start=(j == 0), stop=False)
                            ins = mm(out, v, tl[s][:, (j - a) * P:(j - a + 1) * P], start=False, stop=(j == t))
                        ins.then_inc(turned_used, 1)

            with pe.Fori(0, NPAIR) as i:
                p1a(i)

            def keys(j, first):
                for g in range(4):
                    n, half = g // 2, g % 2
                    pe.wait_ge(page_in[g], key_use(j) * 64 + 64)
                    for a in range(GRAN):
                        t = g * GRAN + a
                        if t >= 2:
                            pe.wait_ge(kct_made, j * 16 + t - 1 + 2)
                        else:
                            pe.wait_ge(so_made, out_use(j) * 2 + 1)
                        b = TURN + t % 2
                        for p in range(NPAIR):
                            ins = tr(bank(b, p * P, (p + 1) * P), cache[g][:, (a * NPAIR + p) * P:(a * NPAIR + p + 1) * P], ident[:, :])
                        ins.then_inc(s_turned, 1)
                        if g and a == 1:
                            logits(j, g - 1)
                logits(j, 3)
                pe.wait_ge(new_z_read, j + 1)
                apart(pe)
                for w in range(NWIN):
                    p = w % NPAIR
                    ins = mm(bank(AVB, 0, SMP), qblk[:, w * P:(w + 1) * P], ks[:, p * SMP:(p + 1) * SMP],
                             start=(w == 0), stop=(w == NWIN - 1))
                ins.then_inc(new_z_full, 1)

            def logits(j, g):
                n, half = g // 2, g % 2
                pe.wait_ge(kct_made, j * 16 + (g + 1) * GRAN + 2)
                if g == 0:
                    pe.wait_ge(s_zc, j + 1)
                    pe.wait_ge(qblk_made, j * 4 + 4)
                for p in range(NPAIR):
                    w = n * NPAIR + p
                    ins = mm(bank(ZB + half), qblk[:, w * P:(w + 1) * P], kct[g % 2][:, p * 512:(p + 1) * 512],
                             start=(w == 0), stop=(w == NWIN - 1))
                ins.then_inc(page_used, 1)

            def values(j, last):
                pe.wait_ge(s_w, j + 1)
                apart(pe)
                for t in range(3):
                    if t < 2:
                        pe.wait_ge(kct_made, newest_keys(j, last) * 16 + 15 + t + 2)
                    else:
                        pe.wait_ge(swt_made, j * 3 + 1)
                    apart(pe)
                    for b in range(GRAN * t, min(GRAN * (t + 1), N_PAGES + 1)):
                        m = P if b < N_PAGES else SMP
                        ins = tr(ps[0:m, (TURN + t % 2) * 512 + (b % GRAN) * P:(TURN + t % 2) * 512 + (b % GRAN) * P + P],
                                 zs_c[:, b * P:b * P + m], ident[:, :])
                    ins.then_inc(s_turned, 1)
                pe.wait_ge(swt_made, j * 3 + 3)
                for n in range(2):
                    out = ps[0:ROWS, n * 512:(n + 1) * 512]
                    for half in range(2):
                        g = 2 * n + half
                        pe.wait_ge(page_in[g], value_use(j, last) * 64 + 64)
                        for a in range(GRAN):
                            at = (half * GRAN + a) * P + n * ROWS
                            ins = mm(out, swT[:, at:at + ROWS], cache[g][:, a * NPAIR * P:(a + 1) * NPAIR * P],
                                     start=(half == 0 and a == 0), stop=False)
                        ins.then_inc(page_used, 1)
                    at = N_PAGES * P + n * ROWS
                    mm(out, swT[0:SMP, at:at + ROWS], vs[:, :], start=False, stop=True).then_inc(so_full, 1)
                for n in range(2):
                    pe.wait_ge(so_copied, j * 2 + n + 1)
                    pe.wait_ge(swt_made, j * 3 + 2 + n)
                    apart(pe)
                    for p in range(NPAIR):
                        ins = tr(bank(TURN + 1 - n, p * ROWS, (p + 1) * ROWS), so[n][:, p * P:(p + 1) * P], ident[0:ROWS, 0:ROWS])
                    ins.then_inc(s_turned, 1)

            p1a_done(pe)
            keys(0, 0)
            with pe.Fori(0, NITER - 1) as j:
                keys(j + 1, None)
                values(j, False)
            values(NITER - 1, True)

            pe.wait_ge(so_made, 2 * NITER + 1)
            base = 6 * NPAIR + 2
            with pe.Fori(0, KT // 2) as j:
                for h in range(2):
                    for k in range(2):
                        n = 3 * h + k
                        pe.wait_ge(w_split, j * 6 + base + n + 1)
                        for c in range(3):
                            d = 6 * h + 3 * k + c
                            pe.wait_ge(gate_free, j * 12 + d + 1)
                            product(bank(d % 2, 0, width_of(c)), wh[n % 2], wl[n % 2], range(KT), xh, xl, CH[c]).then_inc(gate_done, 1)
                    n = 3 * h + 2
                    pe.wait_ge(w_split, j * 6 + base + n + 1)
                    pe.wait_ge(b_lo, 8)
                    for c in range(3):
                        d = 3 * h + c
                        pe.wait_ge(m_made, j * 6 + d + 1 + 1)
                        product(bank(2 + 2 * (d % 2), 0, width_of(c)), wh[n % 2], wl[n % 2], range(4), bh, bl, CH[c])
                        product(bank(3 + 2 * (d % 2), 0, width_of(c)), wh[n % 2], wl[n % 2], range(4, KT), bh, bl, CH[c]).then_inc(proj_done, 1)

            pe.wait_ge(gate_free, 6 * KT + 2)
            pe.wait_ge(m_made, 3 * KT + 3)
            base = 6 * NPAIR + 3 * KT + 2

            def plain_tile(slot, tile_no, first_step, mov_h, mov_l, ready=None):
                pe.wait_ge(w_split, tile_no)
                for c in range(3):
                    pe.wait_ge(step_free, first_step + c + 1)
                    if ready is not None:
                        pe.wait_ge(ready[0], ready[1] + c)
                    product(bank(3 * slot + c, 0, width_of(c)), wh[slot], wl[slot], range(KT), mov_h, mov_l, CH[c]).then_inc(step_done, 1)

            with pe.Fori(0, KT // 2) as j:
                for h in range(2):
                    pe.wait_ge(xin_in, j * 64 + h * 32 + 32)
                    for g in range(3):
                        n = 3 * h + g
                        pe.wait_ge(xt_free, j * 6 + n + 1)
                        apart(pe)
                        for b in range(GRAN * g, min(GRAN * g + GRAN, NB + 1)):
                            m = P if b < NB else SMP
                            ins = tr(bank(6 + n % 2, (b % GRAN) * P, (b % GRAN) * P + m), xin[0:m, b * P:(b + 1) * P], ident[0:m, 0:m])
                        ins.then_inc(xt_turned, 1)
                    plain_tile(h, j * 2 + base + h + 1, j * 6 + 3 * h, mh, ml, (m_lo, 1))
            for c in range(3):
                pe.wait_ge(ssq_made, 3 * KT - 1 + c)
                if c == 0:
                    pe.wait_ge(xt_free, 3 * KT + 2)
                if c == 2:
                    pe.wait_ge(rms_root, 1)
                mm(bank(6 + c % 2, 0, width_of(c)), ones[:, :], ssq[:, CH[c][0]:CH[c][1]], start=True, stop=True).then_inc(rms_sum, 1)
            base += KT
            with pe.Fori(0, NQ) as g:
                with pe.Fori(0, KT // 2) as j:
                    for s in range(2):
                        plain_tile(s, g * (2 * KT) + j * 2 + base + s + 1, g * (6 * KT) + j * 6 + 3 * KT + 3 * s, yh, yl, (y_lo, 3 * KT - 2))
                with pe.Fori(0, KT // 2) as j:
                    for s in range(2):
                        plain_tile(s, g * (2 * KT) + j * 2 + base + KT + s + 1, g * (6 * KT) + j * 6 + 6 * KT + 3 * s, hh, hl,
                                   (h_lo, g * (3 * KT) + 3 * KT - 2))
            for b in range(NB + 1):
                n = P if b < NB else SMP
                if b == 0:
                    pe.wait_ge(step_free, 3 * (KT + 2 * KT * NQ) + 6)
                    pe.wait_ge(rms_made, 3)
                if b >= 4:
                    pe.wait_ge(y_made, b - 3)
                for f in range(KT):
                    at = (b % 4) * 1024 + f * P
                    ins = tr(ps[0:n, at:at + P], x1[:, f * NTOK + b * P:f * NTOK + b * P + n], ident[:, :])
                ins.then_inc(f_turned, 1)

        @block.scalar
        def _(act):
            A = nc.scalar.activation
            with nc.allow_non_contiguous_dma(reason="small constants"):
                act.dma_start(pages[:, :], page_table.rearrange("b n -> (b n)").rearrange("(o n) -> o n", o=1)).then_inc(consts_in, 16)
                act.dma_start(bias_p[:, :], att_bias.to_broadcast([P, NH])).then_inc(consts_in, 16)
                act.dma_start(w2c[:, :], norm2_w.rearrange("o (k p) -> p (o k)", p=P)).then_inc(consts_in, 16)
                for w in range(3):
                    act.dma_start(cw[:, :].rearrange("p (n w) -> p n w", w=3)[:, :, w:w + 1],
                                  conv_w[:, w:w + 1, :].rearrange("o w (n p) -> p n (o w)", p=P)).then_inc(consts_in, 16)

            act.preload_act_table_set("sqrt_and_others")

            def root(b):
                n, r = (P if b < NB else SMP), stat[b]
                act.wait_ge(x_in[b // 2], 16)
                if b == 0:
                    act.wait_ge(const_step, N_EARLY)
                else:
                    act.wait_ge(x_squared, b)
                A(sq0[0:n, :], xr[0:n, b * D:(b + 1) * D], ACT.Square, accum_out=r[0:n, 0:1]).then_inc(x_squared, 1)
                act.wait_ge(x_squared, b + 1)
                A(r[0:n, 1:2], r[0:n, 0:1], ACT.Sqrt, scale=1.0 / D, bias=eps[0:n, 0:1]).then_inc(x_root, 1)

            root(0)
            root(1)
            for b in range(NB + 1):
                if b + 2 <= NB:
                    root(b + 2)
                n, at = (P if b < NB else SMP), X_BANK[b] * 512
                act.wait_ge(x_turned, b + 1)
                A(blocks(xh, NTOK)[:, :, b * P:b * P + n], blocks(ps[:, at:at + D])[:, :, 0:n], ACT.Copy).then_inc(xh_done, 1)
            act.wait_ge(xl_done, NB + 1)
            act.wait_ge(consts_in, 16 * N_CONST)

            def evac(i, d):
                k, (a, z) = d // 3, CH[d % 3]
                if k == Q:
                    z = min(z, SEQ)
                if k in (Q, K):
                    act.wait_ge(dense_done, i * N_DENSE + d + 1)
                    A((qh, kh)[k][:, a:z], bank(d % 3, 0, z - a), ACT.Copy, scale=HD ** -0.5 if k == Q else 1.0).then_inc(evac_hi, 1)

            def p1a(i):
                for e in order:
                    if e[0] in ("dense", "first_half"):
                        if 3 * e[1] + e[2] > 0:
                            evac(i, 3 * e[1] + e[2] - 1)
                    elif e[0] in ("k_out", "v_out"):
                        m = 3 * (e[0] == "v_out") + e[1]
                        s = m % 2
                        act.wait_ge(turn_full, i * N_TURN + turn_no[e] + 1)
                        act.wait_ge(stage_out[s], i * 48 + 16 * (m // 2) + 1)
                        if m >= 5:
                            act.wait_ge(v_made, i * 3 + m - 4)
                        n, w = (P, 512) if e[1] < 2 else (SMP, P)
                        tb = (TURN + turn_no[e] % 2) * 512
                        A(stage[s][0:n, 0:w], ps[0:n, tb:tb + w], ACT.Copy).then_inc(stage_made, 1)
                    elif e[0] == "softplus":
                        u = e[1]
                        act.wait_ge(zc_ready, i * UNITS + u + 1 + 1)
                        A(sp[u % 2][:, 0:width(u)], zc[u % NZ][:, 0:width(u)], ACT.Exp).then_inc(exp_done, 1)
                        act.wait_ge(exp_done, i * UNITS + u + 1)
                        A(sp[u % 2][:, 0:width(u)], sp[u % 2][:, 0:width(u)], ACT.Ln, bias=1.0).then_inc(sp_made, 1)
                    elif e[0] == "weights":
                        u = e[1]
                        act.wait_ge(arg_made, i * UNITS + u + 1)
                        A(zc[u % NZ][:, 0:width(u)], zc[u % NZ][:, 0:width(u)], ACT.Exp).then_inc(w_made, 1)
                    elif e[0] == "turn":
                        u, (a, z) = e[1], groups(e[1])[e[2]]
                        act.wait_ge(turn_full, i * N_TURN + turn_no[e] + 1)
                        act.wait_ge(turned_used, i * N_W + w_no[e] + 1)
                        A(th[w_no[e] % NT][:, 0:(z - a) * P], bank(TURN + turn_no[e] % 2, 0, (z - a) * P), ACT.Copy).then_inc(th_made, 1)
                    elif e[0] == "out":
                        u = e[1]
                        h, t = UNIT[u]
                        if u % 2 == 1:
                            act.wait_ge(turned_used, i * N_W + w_no[("turn", u, len(groups(u)) - 1)] + 1 + NT)
                            act.wait_ge(o_made, i * NB + u // 2 + 1)
                            r, o = slice(h * HD, h * HD + HD), slice(HD - h * HD, 2 * HD - h * HD)
                            A(otmp[r, :], ps[o, AVB * 512:AVB * 512 + 2 * P], ACT.Copy).then_inc(otmp_made, 1)

            act.preload_act_table_set("natural_log_exp_and_others")
            with act.Fori(0, NPAIR) as i:
                p1a(i)

            def keys(j, between=()):
                for t in range(4 * GRAN):
                    for at, f in between:
                        if at == t:
                            f(j - 1)
                    g, a = t // GRAN, t % GRAN
                    if a == 0:
                        act.wait_ge(page_used, key_use(j) * 4 + (g - 1 if g >= 2 else 0) + 4)
                    act.wait_ge(s_turned, j * S_TURNS - turns_before(j) + t + 1)
                    A(blocks(kct[g % 2][:, :], 512)[:, :, a * P:(a + 1) * P], blocks(bank(TURN + t % 2)), ACT.Copy).then_inc(kct_made, 1)

            def softplus(j):
                act.wait_ge(s_zc, j + 1 + 1)
                A(sp_s[:, :], zs_c[:, :], ACT.Exp).then_inc(s_exp, 1)
                act.wait_ge(s_exp, j + 1)
                A(sp_s[:, :], sp_s[:, :], ACT.Ln, bias=1.0).then_inc(s_sp, 1)

            def weights(j):
                act.wait_ge(s_arg, j + 1)
                A(zs_c[:, :], zs_c[:, :], ACT.Exp).then_inc(s_w, 1)

            def values(j, last):
                for t in range(3):
                    n = P if t < 2 else SMP
                    w = 512 if t < 2 else P
                    act.wait_ge(s_turned, s_weights_turned(j, last) + t + 1)
                    A(swT[0:n, t * 512:t * 512 + w], ps[0:n, (TURN + t % 2) * 512:(TURN + t % 2) * 512 + w], ACT.Copy).then_inc(swt_made, 1)
                for n in range(2):
                    act.wait_ge(so_full, j * 2 + n + 1)
                    A(so[n][:, :], ps[0:ROWS, n * 512:(n + 1) * 512], ACT.Copy).then_inc(so_copied, 1)

            p1a_done(act)
            keys(0)
            with act.Fori(0, NITER - 1) as j:
                keys(j + 1, ((3, softplus), (8, weights)))
                values(j, False)
            softplus(NITER - 1)
            weights(NITER - 1)
            values(NITER - 1, True)

            act.wait_ge(so_made, 2 * NITER + 1)
            for k in range(KT):
                A(bh[:, k * NTOK:(k + 1) * NTOK], br[:, k * NTOK:(k + 1) * NTOK], ACT.Copy).then_inc(b_hi, 1)
            with act.Fori(0, KT // 2) as j:
                for h in range(2):
                    for k in range(2):
                        for c in range(3):
                            d = 6 * h + 3 * k + c
                            act.wait_ge(gate_done, j * 12 + d + 1)
                            act.wait_ge(m_made, j * 6 + 3 * h + c + 1)
                            A((sgc, sga)[k][:, CH[c][0]:CH[c][1]], bank(d % 2, 0, CH[c][1] - CH[c][0]), ACT.Sigmoid).then_inc(gate_free, 1)
            act.wait_ge(gate_done, 6 * KT)
            for c in range(3):
                act.wait_ge(m_made, 3 * KT - 3 + c + 1 + 3)
                A(blocks(mh, NTOK)[:, :, CH[c][0]:CH[c][1]], blocks(mg, NTOK)[:, :, CH[c][0]:CH[c][1]], ACT.Copy).then_inc(m_hi, 1)
            act.wait_ge(m_lo, 3)

            with act.Fori(0, KT // 2) as j:
                for h in range(2):
                    f = j * 2 + h
                    for g in range(3):
                        n = 3 * h + g
                        w = 512 if g < 2 else SMP
                        act.wait_ge(xt_turned, j * 6 + n + 1)
                        apart(act)
                        A(x1[:, ds(f * NTOK + g * 512, w)], bank(6 + n % 2, 0, w), ACT.Copy).then_inc(xt_free, 1)
                    for c in range(3):
                        n, (a, z) = 3 * h + c, CH[c]
                        act.wait_ge(step_free, j * 6 + n + 1 + 6)
                        apart(act)
                        A(yh[:, ds(f * NTOK + a, z - a)], x1[:, ds(f * NTOK + a, z - a)], ACT.Copy, scale=w2c[:, ds(f, 1)]).then_inc(y_hi, 1)
                        act.wait_ge(ssq_made, j * 6 + n + 1)
                        apart(act)
                        A(sqt[:, 0:z - a], x1[:, ds(f * NTOK + a, z - a)], ACT.Square).then_inc(sq_made, 1)
            for c in range(3):
                a, z = CH[c]
                act.wait_ge(rms_sum, c + 1)
                if c == 0:
                    act.wait_ge(xt_turned, 3 * KT)
                A(rms[:, a:z], bank(6 + c % 2, 0, z - a), ACT.Sqrt, scale=1.0 / D, bias=eps[:, 0:1]).then_inc(rms_root, 1)
            with act.Fori(0, NQ) as g:
                with act.Fori(0, KT // 2) as j:
                    for n in range(6):
                        s, (a, z) = n % 2, CH[n % 3]
                        no = g * (3 * KT) + j * 6
                        act.wait_ge(step_free, g * (6 * KT) + j * 6 + 3 * KT + n + 1 + 6)
                        A(ts_[s][:, 0:z - a], tt[s][:, 0:z - a], ACT.Square).then_inc(s_made, 1)
                        act.wait_ge(s_made, no + n + 1)
                        apart(act)
                        A(hh[:, ds((j * 2 + n // 3) * NTOK + a, z - a)], ts_[s][:, 0:z - a], ACT.Copy).then_inc(h_hi, 1)
            act.preload_act_table_set("sqrt_and_others")
            for b in range(NB + 1):
                n, r = (P if b < NB else SMP), stat[b]
                act.wait_ge(f_turned, b + 1)
                if b >= 1:
                    act.wait_ge(f_squared, b)
                A(sqf[0:n, :], ps[0:n, (b % 4) * 1024:(b % 4) * 1024 + D], ACT.Square, accum_out=r[0:n, 0:1]).then_inc(f_squared, 1)
                act.wait_ge(f_squared, b + 1)
                A(r[0:n, 1:2], r[0:n, 0:1], ACT.Sqrt, scale=1.0 / D, bias=eps[0:n, 0:1]).then_inc(f_root, 1)

        @block.vector
        def _(v):
            V_ = nc.vector
            v.wait_ge(const_step, N_EARLY)
            V_.tensor_copy(identr[:, :], ident[:, :]).then_inc(identr_made, 1)

            def scale_rows(b):
                n, r = (P if b < NB else SMP), stat[b]
                v.wait_ge(x_root, b + 1)
                V_.reciprocal(r[0:n, 2:3], r[0:n, 1:2]).then_inc(x_rec, 1)
                v.wait_ge(x_rec, b + 1)
                V_.scalar_tensor_tensor(out=xr[0:n, b * D:(b + 1) * D], in0=xr[0:n, b * D:(b + 1) * D], scalar=r[0:n, 2:3],
                                        in1=w1b[0:n, :], op0=ALU.mult, op1=ALU.mult).then_inc(x_scaled, 1)

            v.wait_ge(w1_in, 16)
            scale_rows(0)
            for b in range(NB + 1):
                if b < NB:
                    scale_rows(b + 1)
                n, at = (P if b < NB else SMP), X_BANK[b] * 512
                v.wait_ge(xh_done, b + 1)
                V_.tensor_tensor(blocks(xl, NTOK)[:, :, b * P:b * P + n], blocks(ps[:, at:at + D])[:, :, 0:n],
                                 f32(blocks(xh, NTOK)[:, :, b * P:b * P + n]), ALU.subtract).then_inc(xl_done, 1)
            v.wait_ge(consts_in, 16 * N_CONST)

            SB = 2 + SEQ

            def evac(i, d):
                k, c = d // 3, d % 3
                a, z = CH[c]
                src = bank(c, 0, z - a)
                v.wait_ge(dense_done, i * N_DENSE + d + 1)
                at = i * NTOK
                if k == Q:
                    e = min(z, SEQ)
                    v.wait_ge(evac_hi, i * 6 + d + 1)
                    if c == 2:
                        V_.tensor_scalar(qs[:, ds(i * SMP, SMP)], bank(c, e - a, z - a), HD ** -0.5, None, ALU.mult).then_inc(qs_made, 1)
                    V_.scalar_tensor_tensor(out=ql[:, a:e], in0=bank(c, 0, e - a), scalar=HD ** -0.5, in1=f32(qh[:, a:e]),
                                            op0=ALU.mult, op1=ALU.subtract).then_inc(dense_free, 1)
                elif k == K:
                    v.wait_ge(evac_hi, i * 6 + d + 1)
                    if c == 2:
                        V_.tensor_copy(ks[:, ds(i * SMP, SMP)], bank(c, SEQ - a, z - a)).then_inc(ks_made, 1)
                    V_.tensor_tensor(kl[:, a:z], src, f32(kh[:, a:z]), ALU.subtract).then_inc(dense_free, 1)
                elif k == V:
                    if c == 0:
                        v.wait_ge(cu_out, i * (16 * (1 + NSEQ)) + 1)
                    V_.tensor_copy(vcu[:, a:z], src).then_inc(dense_free, 1)
                elif k == C:
                    V_.tensor_copy(br[:, ds(at + a, z - a)], src).then_inc(dense_free, 1)
                elif k == U:
                    if c == 0:
                        v.wait_ge(turn_full, i * N_TURN + turn_no[("v_out", 2)] + 1)
                        V_.memset(vcu[:, 0:2], 0.0).then_inc(pad_made, 1)
                    e = min(z, SEQ)
                    v.wait_ge(dense_free, i * N_DENSE + 3 * C + 3 + 3)
                    ins = V_.tensor_tensor(vcu[:, 2 + a:2 + e], ps[:, c * 512:c * 512 + e - a], br[:, ds(at + a, e - a)], ALU.mult)
                    if c == 2:
                        ins.then_inc(conv_step, 1)
                        x = c * 512 + e - a
                        ins = V_.tensor_tensor(vcu[:, SB:NV].rearrange("p (b x) -> p b x", x=2 + NEW)[:, :, 2:2 + NEW],
                                               ps[:, x:x + SMP].rearrange("p (b t) -> p b t", t=NEW),
                                               br[:, ds(at + SEQ, SMP)].rearrange("p (b t) -> p b t", t=NEW), ALU.mult)
                    ins.then_inc(dense_free, 1)
                elif k == B:
                    if c == 0:
                        v.wait_ge(conv_step, i * CONV_STEPS + CONV_STEPS)
                    V_.tensor_tensor(br[:, ds(at + a, z - a)], src, br[:, ds(at + a, z - a)], ALU.mult).then_inc(dense_free, 1)

            def conv(i, w):
                if w == 0:
                    v.wait_ge(dense_free, i * N_DENSE + 3 * U + 3 + 3)
                    v.wait_ge(state_in, i * (16 * NSEQ) + 16 * NSEQ)
                    v.wait_ge(pad_made, i + 1)
                    v.wait_ge(conv_step, i * CONV_STEPS + 1)
                wc = cw[:, ds(i * 3 + w, 1)]
                outs = (br[:, ds(i * NTOK, SEQ)], br[:, ds(i * NTOK + SEQ, SMP)].rearrange("p (b t) -> p b t", t=NEW))
                ins_ = (vcu[:, w:w + SEQ], vcu[:, SB:NV].rearrange("p (b x) -> p b x", x=2 + NEW)[:, :, w:w + NEW])
                for q in range(2):
                    if w == 0:
                        op = V_.tensor_scalar(outs[q], ins_[q], wc, None, ALU.mult)
                    else:
                        v.wait_ge(conv_step, i * CONV_STEPS + 1 + 2 * (w - 1) + q + 1)
                        op = V_.scalar_tensor_tensor(out=outs[q], in0=ins_[q], scalar=wc, in1=outs[q], op0=ALU.mult, op1=ALU.add)
                    op.then_inc(conv_step, 1)

            def p1a(i):
                for e in order:
                    if e[0] in ("dense", "first_half"):
                        if 3 * e[1] + e[2] > 0:
                            evac(i, 3 * e[1] + e[2] - 1)
                    elif e[0] == "conv":
                        conv(i, e[1])
                    elif e[0] == "cap":
                        u = e[1]
                        W, h = width(u), UNIT[u][0]
                        v.wait_ge(z_full, i * UNITS + u + 1)
                        bias = bias_p[:, ds(i * 2 + h, 1)]
                        if W > P:
                            V_.tensor_scalar(zc[u % NZ][:, 0:W - P], ps[:, ZB * 512:ZB * 512 + W - P], bias, Z_MAX, ALU.add, ALU.min)
                        V_.scalar_tensor_tensor(out=zc[u % NZ][:, W - P:W], in0=ps[:, ZB * 512 + W - P:ZB * 512 + W], scalar=bias,
                                                in1=diag_cap[:, :], op0=ALU.add, op1=ALU.min).then_inc(zc_ready, 1)
                    elif e[0] == "suffix":
                        u = e[1]
                        W = width(u)
                        rev = sp[u % 2][:, 0:W][:, ::-1]
                        v.wait_ge(sp_made, i * UNITS + u + 1)
                        V_.tensor_tensor_scan(rev, rev, rev, 0.0, ALU.add, ALU.bypass).then_inc(suffix_made, 1)
                        v.wait_ge(suffix_made, i * UNITS + u + 1)
                        V_.tensor_tensor(zc[u % NZ][:, 0:W], zc[u % NZ][:, 0:W], sp[u % 2][:, 0:W], ALU.subtract).then_inc(arg_made, 1)
                    elif e[0] == "low":
                        e = ("turn", *e[1:])
                        (a, z), s = groups(e[1])[e[2]], w_no[e] % NT
                        w = (z - a) * P
                        v.wait_ge(th_made, i * N_W + w_no[e] + 1)
                        V_.tensor_tensor(tl[s][:, 0:w], bank(TURN + turn_no[e] % 2, 0, w), f32(th[s][:, 0:w]), ALU.subtract).then_inc(tl_made, 1)
                    elif e[0] == "v_out":
                        m = 3 + e[1]
                        s = m % 2
                        v.wait_ge(stage_made, i * 6 + m + 1)
                        if e[1] < 2:
                            src = stage[s][:, :].rearrange("p (b h d) -> p b h d", h=2, d=HD)
                            dst = vhl[:, e[1] * GRAN * 2 * P:(e[1] + 1) * GRAN * 2 * P].rearrange("p (b h x d) -> p b h x d", h=2, x=2, d=HD)
                            for h in range(2):
                                V_.tensor_copy(dst[:, :, h, h, :], src[:, :, h, :]).then_inc(vh_made, 1)
                            v.wait_ge(vh_made, i * 4 + 2 * e[1] + 2)
                            V_.tensor_tensor(dst[:, :, 0, 1, :], src[:, :, 0, :], f32(dst[:, :, 0, 0, :]), ALU.subtract)
                            V_.tensor_tensor(dst[:, :, 1, 0, :], src[:, :, 1, :], f32(dst[:, :, 1, 1, :]), ALU.subtract).then_inc(v_made, 1)
                        else:
                            V_.tensor_copy(vs[:, ds(i * P, P)], stage[s][0:SMP, 0:P]).then_inc(v_made, 1)
                    elif e[0] == "out":
                        u = e[1]
                        h, t = UNIT[u]
                        if u % 2 == 1:
                            r = slice(h * HD, h * HD + HD)
                            v.wait_ge(otmp_made, i * NB + u // 2 + 1)
                            V_.tensor_tensor(br[r, ds(i * NTOK + (4 * NTOK + t // 2 * (2 * P)), 2 * P)], ps[r, AVB * 512:AVB * 512 + 2 * P],
                                             otmp[r, :], ALU.add).then_inc(o_made, 1)
                evac(i, N_DENSE - 1)

            with v.Fori(0, NPAIR) as i:
                p1a(i)

            def own_q(j):
                for n in range(2):
                    for h in range(2):
                        r = slice(h * HD, h * HD + HD)
                        dst = qblk[r, n * NPAIR * WIN:(n + 1) * NPAIR * WIN].rearrange("p (w x) -> p w x", x=WIN)[:, :, h * NEW:h * NEW + NEW]
                        src = qs[r, :].rearrange("p (w x) -> p w x", x=SMP)[:, :, ds(j * (2 * NEW) + n * NEW, NEW)]
                        V_.tensor_copy(dst, src).then_inc(qblk_made, 1)

            def capped(j):
                v.wait_ge(new_z_full, j + 1)
                V_.scalar_tensor_tensor(out=zs_c[:, PAST:KEYS], in0=bank(AVB, 0, SMP), scalar=bias_s[:, 0:1],
                                        in1=new_cap[:, ds(j * SMP, SMP)], op0=ALU.add, op1=ALU.min).then_inc(new_z_read, 1)
                V_.tensor_scalar(zs_c[:, 0:PAST], ps[:, ZB * 512:ZB * 512 + PAST], bias_s[:, 0:1], Z_MAX,
                                 ALU.add, ALU.min).then_inc(s_zc, 1)

            def suffix(j):
                rev = sp_s[:, :][:, ::-1]
                v.wait_ge(s_sp, j + 1)
                V_.tensor_tensor_scan(rev, rev, rev, 0.0, ALU.add, ALU.bypass).then_inc(s_suffix, 1)
                v.wait_ge(s_suffix, j + 1)
                V_.tensor_tensor(zs_c[:, :], zs_c[:, :], sp_s[:, :], ALU.subtract).then_inc(s_arg, 1)

            def values(j, last):
                for n in range(2):
                    v.wait_ge(s_turned, s_weights_turned(j, last) + 3 + n + 1)
                    for h in range(2):
                        r = slice(h * HD, h * HD + HD)
                        step_ = ROWS + 2 * NEW
                        src = ps[r, (TURN + 1 - n) * 512:(TURN + 1 - n) * 512 + NPAIR * step_].rearrange("p (w x) -> p w x", x=step_)[:, :, h * NEW:h * NEW + NEW]
                        dst = blocks(br[r, :], NTOK)[:, NPAIR:2 * NPAIR, ds(j * (2 * NEW) + (SEQ + n * NEW), NEW)]
                        ins = V_.tensor_copy(dst, src)
                    ins.then_inc(so_made, 1)

            p1a_done(v)
            v.wait_ge(bias_in, 16 * (P // NEW))
            v.wait_ge(const_step, N_STEPS)
            V_.memset(qblk[:, :], 0.0).then_inc(qblk_zero, 1)
            v.wait_ge(qblk_zero, 1)
            own_q(0)
            with v.Fori(0, NITER - 1) as j:
                capped(j)
                own_q(j + 1)
                suffix(j)
                values(j, False)
            capped(NITER - 1)
            suffix(NITER - 1)
            values(NITER - 1, True)

            for k in range(KT):
                x = slice(k * NTOK, (k + 1) * NTOK)
                v.wait_ge(b_hi, k + 1)
                V_.tensor_tensor(bl[:, x], br[:, x], f32(bh[:, x]), ALU.subtract).then_inc(b_lo, 1)
            v.wait_ge(b_lo, KT)
            with v.Fori(0, KT // 2) as j:
                for h in range(2):
                    for c in range(3):
                        d, (a, z) = 3 * h + c, CH[c]
                        w = z - a
                        m = mg[:, ds(j * (2 * NTOK) + (h * NTOK + a), w)]
                        v.wait_ge(proj_done, j * 6 + d + 1)
                        v.wait_ge(gate_free, j * 12 + 6 * h + c + 3 + 1 + 2)
                        V_.tensor_tensor(m, bank(2 + 2 * (d % 2), 0, w), sgc[:, a:z], ALU.mult).then_inc(gated_c, 1)
                        V_.tensor_tensor(sga[:, a:z], bank(3 + 2 * (d % 2), 0, w), sga[:, a:z], ALU.mult).then_inc(gated_a, 1)
                        v.wait_ge(gated_c, j * 6 + d + 1)
                        v.wait_ge(gated_a, j * 6 + d + 1)
                        V_.tensor_tensor(m, m, sga[:, a:z], ALU.add).then_inc(m_made, 1)
            for c in range(3):
                a, z = CH[c]
                v.wait_ge(m_hi, c + 1)
                V_.tensor_tensor(blocks(ml, NTOK)[:, :, a:z], blocks(mg, NTOK)[:, :, a:z], f32(blocks(mh, NTOK)[:, :, a:z]),
                                 ALU.subtract).then_inc(m_lo, 1)

            V_.memset(ssq[:, :], 0.0).then_inc(ssq_made, 1)
            with v.Fori(0, KT // 2) as j:
                for h in range(2):
                    f = j * 2 + h
                    for c in range(3):
                        n, (a, z) = 3 * h + c, CH[c]
                        x = x1[:, ds(f * NTOK + a, z - a)]
                        y = ds(f * NTOK + a, z - a)
                        v.wait_ge(xt_free, j * 6 + 3 * h + 3 + 2)
                        v.wait_ge(step_done, j * 6 + n + 1)
                        V_.tensor_tensor(x, bank(n, 0, z - a), x, ALU.add).then_inc(step_free, 1)
                        v.wait_ge(step_free, j * 6 + n + 1 + 6)
                        v.wait_ge(y_hi, j * 6 + n + 1)
                        V_.scalar_tensor_tensor(out=yl[:, y], in0=x, scalar=w2c[:, ds(f, 1)], in1=f32(yh[:, y]),
                                                op0=ALU.mult, op1=ALU.subtract).then_inc(y_lo, 1)
                        v.wait_ge(sq_made, j * 6 + n + 1)
                        v.wait_ge(ssq_made, j * 6 + n + 1)
                        V_.tensor_tensor(ssq[:, a:z], ssq[:, a:z], sqt[:, 0:z - a], ALU.add).then_inc(ssq_made, 1)
            for c in range(3):
                a, z = CH[c]
                v.wait_ge(rms_root, c + 1)
                V_.reciprocal(rms[:, a:z], rms[:, a:z]).then_inc(rms_made, 1)
            v.wait_ge(rms_made, 3)

            with v.Fori(0, NQ) as g:
                with v.Fori(0, KT // 2) as j:
                    def low(n):
                        a, z = CH[n % 3]
                        y = ds((j * 2 + n // 3) * NTOK + a, z - a)
                        v.wait_ge(h_hi, g * (3 * KT) + j * 6 + n + 1)
                        V_.tensor_tensor(hl[:, y], ts_[n % 2][:, 0:z - a], f32(hh[:, y]), ALU.subtract).then_inc(h_lo, 1)

                    for n in range(6):
                        a, z = CH[n % 3]
                        v.wait_ge(step_done, g * (6 * KT) + j * 6 + 3 * KT + n + 1)
                        V_.scalar_tensor_tensor(out=tt[n % 2][:, 0:z - a], in0=bank(n, 0, z - a), scalar=0.0, in1=rms[:, a:z],
                                                op0=ALU.max, op1=ALU.mult).then_inc(step_free, 1)
                        if n >= 1:
                            low(n - 1)
                    low(5)
                with v.Fori(0, KT // 2) as j:
                    for n in range(6):
                        a, z = CH[n % 3]
                        x = x1[:, ds((j * 2 + n // 3) * NTOK + a, z - a)]
                        v.wait_ge(step_done, g * (6 * KT) + j * 6 + 6 * KT + n + 1)
                        V_.tensor_tensor(x, bank(n, 0, z - a), x, ALU.add).then_inc(step_free, 1)

            v.wait_ge(wf_in, 16)
            for b in range(NB + 1):
                n, r, s = (P if b < NB else SMP), stat[b], b % NY
                v.wait_ge(f_root, b + 1)
                V_.reciprocal(r[0:n, 2:3], r[0:n, 1:2]).then_inc(f_rec, 1)
                v.wait_ge(f_rec, b + 1)
                if b >= NY:
                    v.wait_ge(y_out[s], 16 * (b // NY))
                V_.scalar_tensor_tensor(out=yst[s][0:n, :], in0=ps[0:n, (b % 4) * 1024:(b % 4) * 1024 + D], scalar=r[0:n, 2:3],
                                        in1=wfb[0:n, :], op0=ALU.mult, op1=ALU.mult).then_inc(y_made, 1)


INPUTS = ["x_prompt", "x_sample", "cache_k", "cache_v", "state_conv", "page_table", "norm1_w", "w_in", "conv_w",
          "w_proj_conv", "w_proj_attn", "att_bias", "w_out", "norm2_w", "w_up", "w_down", "norm_f_w"]


def kernel(**inputs):
    import numpy as np
    import concourse.bacc as bacc
    from concourse.bass_utils import run_bass_kernel_spmd as run

    xp, xs, page = inputs["x_prompt"].shape, inputs["x_sample"].shape, inputs["cache_k"].shape
    dc = inputs["state_conv"].shape[3]
    paged = (1, xp[0], xp[1] // page[2], page[2], page[3], page[4])
    new = (1, xs[0], xs[1], page[3], page[4])
    shapes = [("y_prompt", xp), ("y_sample", xs), ("k_prompt", paged), ("v_prompt", paged), ("conv_prompt", (1, xp[0], 2, dc)),
              ("k_sample", new), ("v_sample", new), ("conv_sample", (1, xs[0], 2, dc))]
    nc = bacc.Bacc("TRN2", target_bir_lowering=False, num_devices=1)
    arrays, args = {}, []
    for name in INPUTS:
        a = np.ascontiguousarray(inputs[name])
        arrays["in_" + name] = a
        args.append(nc.dram_tensor("in_" + name, a.shape, mybir.dt.from_np(a.dtype), kind="ExternalInput").ap())
    for name, shape in shapes:
        args.append(nc.dram_tensor("out_" + name, shape, F32, kind="ExternalOutput").ap())
    hybrid_layer(nc, *args)
    r = run(nc, [arrays], core_ids=[0])
    return tuple(r.results[0]["out_" + name] for name, _ in shapes)
```
